# Optimizing a Trainium2 kernel written in Bass

```python
import math
import jax, jax.numpy as jnp
from jax import lax
import numpy as np

D_MODEL = 1024
BATCH = 1
SEQ = 1024
DEPTH = 2
DEC_BATCH = 1
DEC_SEQ = 32
PAST_LEN = 256

CHUNK = 64
Q_BLOCK = 128
N_A_LAYERS = DEPTH // 2
N_B_LAYERS = DEPTH - N_A_LAYERS
ALPHA = (2.0 * DEPTH) ** 0.25
BETA = (8.0 * DEPTH) ** -0.25
LN_EPS = 1e-5
RMS_EPS = 1e-6
GDN_HEADS = 8
GDN_DK = 128
GDN_DV = 128
GDN_CONV = 4
GDN_QK = GDN_HEADS * GDN_DK
GDN_V = GDN_HEADS * GDN_DV
GDN_CONV_CH = 2 * GDN_QK + GDN_V
GDN_PROJ = 2 * GDN_QK + 2 * GDN_V + 2 * GDN_HEADS
MLA_HEADS = 8
MLA_NOPE = 128
MLA_ROPE = 64
MLA_V = 128
MLA_KV_LORA = 256
MLA_Q_LORA = 384
ROPE_THETA = 10000.0
MLA_SCALE = (MLA_NOPE + MLA_ROPE) ** -0.5
D_FF = 2816
FFN_CONV = 3

kernel_name = 'hybrid_gdn_mla_streaming_step'

def layer_norm(x, g, b):
    xf = x.astype(jnp.float32)
    mu = jnp.mean(xf, axis=-1, keepdims=True)
    var = jnp.mean(jnp.square(xf - mu), axis=-1, keepdims=True)
    return ((xf - mu) * lax.rsqrt(var + LN_EPS) * g + b).astype(x.dtype)

def rms_norm(x, g):
    xf = x.astype(jnp.float32)
    return (xf * lax.rsqrt(jnp.mean(xf * xf, axis=-1, keepdims=True) + RMS_EPS) * g).astype(x.dtype)

def l2_normalize(x):
    return x * lax.rsqrt(jnp.sum(x * x, axis=-1, keepdims=True) + RMS_EPS)

def causal_dwconv(u, hist, w):
    K = w.shape[0]
    L = u.shape[1]
    full = jnp.concatenate([hist.astype(u.dtype), u], axis=1)
    out = full[:, 0:L] * w[0]
    for j in range(1, K):
        out = out + full[:, j:j + L] * w[j]
    return out, full[:, full.shape[1] - (K - 1):]

def rope_tables(pos):
    inv = 1.0 / (ROPE_THETA ** (jnp.arange(0, MLA_ROPE, 2, dtype=jnp.float32) / MLA_ROPE))
    ang = pos.astype(jnp.float32)[:, None] * inv[None, :]
    ang = jnp.concatenate([ang, ang], axis=-1)
    return jnp.cos(ang), jnp.sin(ang)

def apply_rope(x, cos, sin):
    xf = x.astype(jnp.float32)
    x1, x2 = jnp.split(xf, 2, axis=-1)
    rot = jnp.concatenate([-x2, x1], axis=-1)
    return (xf * cos + rot * sin).astype(x.dtype)

def ada_terms(c, w, b):
    m = jax.nn.silu(c) @ w + b
    shift, scale, gate = jnp.split(m, 3, axis=-1)
    return shift[:, None], scale[:, None], gate[:, None]

def gdn_chunk_step(S, inp):
    q, k, v, g, beta = inp
    C = q.shape[2]
    G = jnp.cumsum(g, axis=-1)
    idx = jnp.arange(C)
    incl = idx[:, None] >= idx[None, :]
    strict = idx[:, None] > idx[None, :]
    gam = jnp.exp(jnp.where(incl, G[..., :, None] - G[..., None, :], -jnp.inf))
    kk = jnp.einsum('bhik,bhjk->bhij', k, k)
    a_mat = jnp.where(strict, beta[..., :, None] * kk * gam, 0.0)
    eG = jnp.exp(G)[..., None]
    rhs = jnp.concatenate([beta[..., None] * v, beta[..., None] * k * eG], axis=-1)
    sol = lax.linalg.triangular_solve(jnp.eye(C, dtype=jnp.float32) + a_mat, rhs,
                                      left_side=True, lower=True, unit_diagonal=True)
    u, w = sol[..., :GDN_DV], sol[..., GDN_DV:]
    v_new = u - jnp.einsum('bhck,bhkv->bhcv', w, S)
    qk = jnp.einsum('bhik,bhjk->bhij', q, k) * gam
    o = jnp.einsum('bhck,bhkv->bhcv', q * eG, S) + jnp.einsum('bhij,bhjv->bhiv', qk, v_new)
    g_last = G[..., -1]
    k_dec = k * jnp.exp(g_last[..., None] - G)[..., None]
    S_new = jnp.exp(g_last)[..., None, None] * S + jnp.einsum('bhck,bhcv->bhkv', k_dec, v_new)
    return S_new, o

def gdn_mixer(h, conv_hist, S0, w_in, conv_w, a_log, dt_bias, norm_g, w_out):
    B, L, _ = h.shape
    proj = h @ w_in
    qkv = proj[..., :GDN_CONV_CH]
    z = proj[..., GDN_CONV_CH:GDN_CONV_CH + GDN_V]
    b_raw = proj[..., GDN_CONV_CH + GDN_V:GDN_CONV_CH + GDN_V + GDN_HEADS]
    a_raw = proj[..., GDN_CONV_CH + GDN_V + GDN_HEADS:]
    qkv, new_hist = causal_dwconv(qkv, conv_hist, conv_w)
    qkv = jax.nn.silu(qkv.astype(jnp.float32))
    q = qkv[..., :GDN_QK].reshape(B, L, GDN_HEADS, GDN_DK)
    k = qkv[..., GDN_QK:2 * GDN_QK].reshape(B, L, GDN_HEADS, GDN_DK)
    v = qkv[..., 2 * GDN_QK:].reshape(B, L, GDN_HEADS, GDN_DV)
    q = l2_normalize(q) * (GDN_DK ** -0.5)
    k = l2_normalize(k)
    beta = jax.nn.sigmoid(b_raw.astype(jnp.float32))
    g = -jnp.exp(a_log.astype(jnp.float32)) * jax.nn.softplus(a_raw.astype(jnp.float32) + dt_bias.astype(jnp.float32))
    c_len = CHUNK if L % CHUNK == 0 else L
    n = L // c_len

    def to_chunks(t):
        t = jnp.moveaxis(t.reshape(B, n, c_len, *t.shape[2:]), 1, 0)
        return jnp.swapaxes(t, 2, 3)

    S_end, o = lax.scan(gdn_chunk_step, S0.astype(jnp.float32),
                        (to_chunks(q), to_chunks(k), to_chunks(v), to_chunks(g), to_chunks(beta)))
    o = jnp.moveaxis(jnp.swapaxes(o, 2, 3), 0, 1).reshape(B, L, GDN_HEADS, GDN_DV)
    o = rms_norm(o, norm_g.astype(jnp.float32)) * jax.nn.silu(z.reshape(B, L, GDN_HEADS, GDN_DV).astype(jnp.float32))
    out = o.reshape(B, L, GDN_V).astype(h.dtype) @ w_out
    return out, new_hist, S_end.astype(S0.dtype)

def chunk_causal_attention(q_nope, q_pe, k_nope, k_pe, v, q_pos, k_pos):
    B, Lq, H, _ = q_nope.shape
    k_chunk = k_pos // CHUNK

    def block(args):
        qn, qp, qpos = args
        s = jnp.einsum('bqhn,bkhn->bhqk', qn, k_nope) + jnp.einsum('bqhr,bkr->bhqk', qp, k_pe)
        s = s.astype(jnp.float32) * MLA_SCALE
        allowed = k_chunk[None, :] <= (qpos // CHUNK)[:, None]
        p = jax.nn.softmax(jnp.where(allowed, s, -jnp.inf), axis=-1).astype(v.dtype)
        return jnp.einsum('bhqk,bkhv->bqhv', p, v)

    if Lq % Q_BLOCK == 0 and Lq > Q_BLOCK:
        nb = Lq // Q_BLOCK
        split = lambda t: jnp.moveaxis(t.reshape(B, nb, Q_BLOCK, *t.shape[2:]), 1, 0)
        out = lax.map(block, (split(q_nope), split(q_pe), q_pos.reshape(nb, Q_BLOCK)))
        return jnp.moveaxis(out, 0, 1).reshape(B, Lq, H, MLA_V)
    return block((q_nope, q_pe, q_pos))

def trunk(x, c, gdn_state, gdn_conv, ffn_conv, ckv_past, kpe_past, p):
    B, L, _ = x.shape
    past = kpe_past.shape[1]
    q_pos = past + jnp.arange(L, dtype=jnp.int32)
    k_pos = jnp.arange(past + L, dtype=jnp.int32)
    cos, sin = rope_tables(q_pos)
    gdn_S_out, gdn_conv_out, ffn_conv_out = [], [], []
    ckv_new = kpe_new = k_nope = v_all = kpe_all = None
    for layer in range(DEPTH):
        shift, scale, gate = ada_terms(c, p['ada_w'][2 * layer], p['ada_b'][2 * layer])
        hin = x * (1.0 + scale) + shift
        if layer < N_A_LAYERS:
            mix, hist, S = gdn_mixer(hin, gdn_conv[:, layer], gdn_state[:, layer],
                                     p['gdn_w_in'][layer], p['gdn_conv_w'][layer], p['gdn_a_log'][layer],
                                     p['gdn_dt_bias'][layer], p['gdn_norm_g'][layer], p['gdn_w_out'][layer])
            gdn_S_out.append(S)
            gdn_conv_out.append(hist)
        else:
            if layer == N_A_LAYERS:
                kv = x @ p['kv_w_down']
                ckv_new = rms_norm(kv[..., :MLA_KV_LORA], p['kv_norm_g'])
                kpe_new = apply_rope(kv[..., MLA_KV_LORA:], cos, sin)
                ckv_all = jnp.concatenate([ckv_past.astype(x.dtype), ckv_new], axis=1)
                kpe_all = jnp.concatenate([kpe_past.astype(x.dtype), kpe_new], axis=1)
                kv_up = (ckv_all @ p['kv_w_up']).reshape(B, past + L, MLA_HEADS, MLA_NOPE + MLA_V)
                k_nope, v_all = kv_up[..., :MLA_NOPE], kv_up[..., MLA_NOPE:]
            j = layer - N_A_LAYERS
            q = rms_norm(hin @ p['mla_w_dq'][j], p['mla_q_norm_g'][j]) @ p['mla_w_uq'][j]
            q = q.reshape(B, L, MLA_HEADS, MLA_NOPE + MLA_ROPE)
            q_pe = apply_rope(q[..., MLA_NOPE:], cos[:, None], sin[:, None])
            o = chunk_causal_attention(q[..., :MLA_NOPE], q_pe, k_nope, kpe_all, v_all, q_pos, k_pos)
            mix = o.reshape(B, L, MLA_HEADS * MLA_V) @ p['mla_w_out'][j]
        x = layer_norm(ALPHA * x + (1.0 + gate) * mix, p['ln_g'][2 * layer], p['ln_b'][2 * layer])
        shift, scale, gate = ada_terms(c, p['ada_w'][2 * layer + 1], p['ada_b'][2 * layer + 1])
        hin = x * (1.0 + scale) + shift
        u = hin @ p['ffn_w_in'][layer] + p['ffn_b_in'][layer]
        u, hist = causal_dwconv(u, ffn_conv[:, layer], p['ffn_conv_w'][layer])
        u = u + p['ffn_conv_b'][layer]
        ffn_conv_out.append(hist)
        f = (jax.nn.silu(u[..., :D_FF]) * u[..., D_FF:]) @ p['ffn_w_down'][layer]
        x = layer_norm(ALPHA * x + (1.0 + gate) * f, p['ln_g'][2 * layer + 1], p['ln_b'][2 * layer + 1])
    return (x, jnp.stack(gdn_S_out, axis=1), jnp.stack(gdn_conv_out, axis=1),
            jnp.stack(ffn_conv_out, axis=1), ckv_new, kpe_new)

def setup_inputs(seed: int = 0) -> dict:
    key = jax.random.key(seed)
    keys = iter(jax.random.split(key, 64))
    f32 = jnp.float32

    def nrm(shape, scale):
        return scale * jax.random.normal(next(keys), shape, f32)

    def unif(shape, lo, hi):
        return jax.random.uniform(next(keys), shape, f32, lo, hi)

    D = D_MODEL
    return {
        'x_prompt': nrm((BATCH, SEQ, D), 1.0),
        'x_sample': nrm((DEC_BATCH, DEC_SEQ, D), 1.0),
        'c_prompt': nrm((BATCH, D), 1.0),
        'c_sample': nrm((DEC_BATCH, D), 1.0),
        'state_gdn': nrm((DEC_BATCH, N_A_LAYERS, GDN_HEADS, GDN_DK, GDN_DV), 0.1),
        'state_gdn_conv': nrm((DEC_BATCH, N_A_LAYERS, GDN_CONV - 1, GDN_CONV_CH), 1.0),
        'state_ffn_conv': nrm((DEC_BATCH, DEPTH, FFN_CONV - 1, 2 * D_FF), 1.0),
        'cache_ckv': nrm((DEC_BATCH, PAST_LEN, MLA_KV_LORA), 1.0),
        'cache_kpe': nrm((DEC_BATCH, PAST_LEN, MLA_ROPE), 1.0),
        'ada_w': nrm((2 * DEPTH, D, 3 * D), 0.1 * D ** -0.5),
        'ada_b': nrm((2 * DEPTH, 3 * D), 0.02),
        'ln_g': 1.0 + nrm((2 * DEPTH, D), 0.02),
        'ln_b': nrm((2 * DEPTH, D), 0.02),
        'gdn_w_in': nrm((N_A_LAYERS, D, GDN_PROJ), D ** -0.5),
        'gdn_conv_w': nrm((N_A_LAYERS, GDN_CONV, GDN_CONV_CH), GDN_CONV ** -0.5),
        'gdn_a_log': jnp.log(unif((N_A_LAYERS, GDN_HEADS), 1.0, 16.0)),
        'gdn_dt_bias': unif((N_A_LAYERS, GDN_HEADS), -4.0, -1.0),
        'gdn_norm_g': 1.0 + nrm((N_A_LAYERS, GDN_DV), 0.02),
        'gdn_w_out': nrm((N_A_LAYERS, GDN_V, D), BETA * GDN_V ** -0.5),
        'kv_w_down': nrm((D, MLA_KV_LORA + MLA_ROPE), D ** -0.5),
        'kv_norm_g': 1.0 + nrm((MLA_KV_LORA,), 0.02),
        'kv_w_up': nrm((MLA_KV_LORA, MLA_HEADS * (MLA_NOPE + MLA_V)), MLA_KV_LORA ** -0.5),
        'mla_w_dq': nrm((N_B_LAYERS, D, MLA_Q_LORA), D ** -0.5),
        'mla_q_norm_g': 1.0 + nrm((N_B_LAYERS, MLA_Q_LORA), 0.02),
        'mla_w_uq': nrm((N_B_LAYERS, MLA_Q_LORA, MLA_HEADS * (MLA_NOPE + MLA_ROPE)), MLA_Q_LORA ** -0.5),
        'mla_w_out': nrm((N_B_LAYERS, MLA_HEADS * MLA_V, D), BETA * (MLA_HEADS * MLA_V) ** -0.5),
        'ffn_w_in': nrm((DEPTH, D, 2 * D_FF), D ** -0.5),
        'ffn_b_in': nrm((DEPTH, 2 * D_FF), 0.02),
        'ffn_conv_w': nrm((DEPTH, FFN_CONV, 2 * D_FF), FFN_CONV ** -0.5),
        'ffn_conv_b': nrm((DEPTH, 2 * D_FF), 0.02),
        'ffn_w_down': nrm((DEPTH, D_FF, D), BETA * D_FF ** -0.5),
    }

def reference(x_prompt, x_sample, c_prompt, c_sample, state_gdn, state_gdn_conv, state_ffn_conv,
              cache_ckv, cache_kpe, ada_w, ada_b, ln_g, ln_b, gdn_w_in, gdn_conv_w, gdn_a_log,
              gdn_dt_bias, gdn_norm_g, gdn_w_out, kv_w_down, kv_norm_g, kv_w_up, mla_w_dq,
              mla_q_norm_g, mla_w_uq, mla_w_out, ffn_w_in, ffn_b_in, ffn_conv_w, ffn_conv_b, ffn_w_down):
    p = {'ada_w': ada_w, 'ada_b': ada_b, 'ln_g': ln_g, 'ln_b': ln_b,
         'gdn_w_in': gdn_w_in, 'gdn_conv_w': gdn_conv_w, 'gdn_a_log': gdn_a_log,
         'gdn_dt_bias': gdn_dt_bias, 'gdn_norm_g': gdn_norm_g, 'gdn_w_out': gdn_w_out,
         'kv_w_down': kv_w_down, 'kv_norm_g': kv_norm_g, 'kv_w_up': kv_w_up,
         'mla_w_dq': mla_w_dq, 'mla_q_norm_g': mla_q_norm_g, 'mla_w_uq': mla_w_uq, 'mla_w_out': mla_w_out,
         'ffn_w_in': ffn_w_in, 'ffn_b_in': ffn_b_in, 'ffn_conv_w': ffn_conv_w,
         'ffn_conv_b': ffn_conv_b, 'ffn_w_down': ffn_w_down}
    bp = x_prompt.shape[0]
    z_gdn = jnp.zeros((bp,) + state_gdn.shape[1:], state_gdn.dtype)
    z_gconv = jnp.zeros((bp,) + state_gdn_conv.shape[1:], state_gdn_conv.dtype)
    z_fconv = jnp.zeros((bp,) + state_ffn_conv.shape[1:], state_ffn_conv.dtype)
    z_ckv = jnp.zeros((bp, 0, MLA_KV_LORA), cache_ckv.dtype)
    z_kpe = jnp.zeros((bp, 0, MLA_ROPE), cache_kpe.dtype)
    y_prompt, p_gdn, p_gconv, p_fconv, p_ckv, p_kpe = trunk(
        x_prompt, c_prompt, z_gdn, z_gconv, z_fconv, z_ckv, z_kpe, p)
    y_sample, s_gdn, s_gconv, s_fconv, s_ckv, s_kpe = trunk(
        x_sample, c_sample, state_gdn, state_gdn_conv, state_ffn_conv, cache_ckv, cache_kpe, p)
    return (y_prompt, y_sample, p_gdn, p_gconv, p_fconv, p_ckv, p_kpe,
            s_gdn, s_gconv, s_fconv, s_ckv, s_kpe)


_drawn_inputs = setup_inputs


def setup_inputs(seed=0):
    import zlib

    import numpy as np

    out = dict(_drawn_inputs(seed))
    spreads = {}
    factors = {'cache_kpe': 3.342,
     'gdn_norm_g': 8.0,
     'kv_norm_g': 2.903,
     'mla_q_norm_g': 8.0,
     'ffn_b_in': 2.791,
     'ffn_conv_b': 6.528}
    for name, (base, spread) in spreads.items():
        noise = np.random.default_rng([zlib.crc32(name.encode()), seed]).standard_normal(out[name].shape)
        drawn = base * np.exp(spread * noise) if base else spread * noise
        out[name] = __import__('jax').numpy.asarray(drawn.astype(out[name].dtype))
    for name, factor in factors.items():
        out[name] = (out[name] * factor).astype(out[name].dtype)
    return out
```

```python
import math
from contextlib import ExitStack

import concourse.bass as bass
from concourse import mybir

D = 1024
KB = D // 128
SEQ, DEC, PAST = 1024, 32, 256
GAP = 4
SAM = SEQ + GAP
T = SAM + DEC
CHS = [(0, 354), (354, 354), (708, 352)]
NCH = len(CHS)
CW = 354
HEADS = 8
GT = SEQ // 128
CHUNK = 64
QKVB = 24
ZB = 8
FB = 22
GC, FC = 4, 3
DEPTH = 2
ALPHA = (2.0 * DEPTH) ** 0.25
LN_EPS, RMS_EPS = 1e-5, 1e-6
NSUB = 4
ADAM = 24
SLAB = 1024
LEVELS = (2, 4, 8, 16, 32)
NEG = -1e30

S_A = 0
S_WO = S_A + QKVB + ZB + 1
S_F0 = S_WO + KB
NF = 3 * FB
S_KV = S_F0 + NF
S_DQ = S_KV + 3
S_QP = S_DQ + 3
S_HD = S_QP + 2
S_MO = S_HD + HEADS
S_F1 = S_MO + KB
NSLAB = S_F1 + NF

P_ADAB = 0
P_LNG = P_ADAB + NSUB * ADAM
P_LNB = P_LNG + NSUB * KB
P_GCV = P_LNB + NSUB * KB
GPW = GC + GC - 1
P_FFN = P_GCV + QKVB * GPW
FPW = 2 * 7
P_GNG = P_FFN + DEPTH * FB * FPW
P_KVG = P_GNG + 1
P_QG = P_KVG + 2
P_ALOG = P_QG + 3
P_DTB = P_ALOG + 8
NPAR = P_DTB + 8

C_ID, C_ONE, C_CUM, C_SAME, C_IND0, C_IND1, C_NEG, C_SELC, C_ROT, C_MASK = range(10)
NCST = C_MASK + 6
KEYS = T + PAST
NOPE, ROPE, LORA, QLORA = 128, 64, 256, 384
LB, QB = LORA // 128, QLORA // 128
SCALE = (NOPE + ROPE) ** -0.5
SKEYS = KEYS - SAM
KPAD = SAM + 128 * (-(-SKEYS // 128))
KCH = CHS + [(T, PAST)]
THETA = 10000.0


def constants():
    import numpy as np
    j = np.arange(128)[:, None]
    i = np.arange(128)[None, :]
    same = (j // CHUNK) == (i // CHUNK)
    c = np.zeros((NCST, 128, 128), np.float32)
    c[C_ID] = np.eye(128)
    c[C_ONE] = 1.0
    c[C_CUM] = same & (j <= i)
    c[C_SAME] = same
    c[C_IND0] = (j < CHUNK) & (i >= 0)
    c[C_IND1] = (j >= CHUNK) & (i >= 0)
    c[C_SELC] = (i % 8 == i // 8) & (i < 64) & (j >= 0)
    half = ROPE // 2
    c[C_ROT] = np.where(j == i + half, -1.0, 0.0) * ((i % ROPE) < half) + np.where(j == i - half, 1.0, 0.0) * ((i % ROPE) >= half)
    c[C_NEG] = np.where(same & (j <= i), 0.0, NEG)
    for n, s in enumerate((1,) + LEVELS):
        c[C_MASK + n] = ((i // s) % 2 == 1) & (j // s == i // s - 1)
    return np.ascontiguousarray(c.transpose(1, 0, 2))


def tables():
    import numpy as np
    pos = np.concatenate([np.arange(SEQ), np.zeros(GAP), PAST + np.arange(DEC)]).astype(np.float32)
    inv = (1.0 / (np.float32(THETA) ** (np.arange(0, ROPE, 2, dtype=np.float32) / np.float32(ROPE)))).astype(np.float32)
    ang = (pos[None, :] * np.tile(inv, 4)[:, None]).astype(np.float32)
    cs = np.stack([np.cos(ang), np.sin(ang)], 1).astype(np.float32)
    rows = np.zeros((8, 8, 128), np.float32)
    rows[np.arange(8), np.arange(8)] = 1.0
    m = np.zeros((1, 2, 128), np.float32)
    m[0, 0, :CHUNK] = 1.0
    m[0, 1, CHUNK:] = NEG
    return np.ascontiguousarray(cs), rows, m


def build(nc, xT, cT, cB, ws, wada0, wada, par, cst, s0, cs, rows, msk, pckv, pkpe, y, o_gdn, o_gcv, s_gdn, o_fcv, o_ckv, o_kpe):
    fp32, f32r = mybir.dt.float32, mybir.dt.float32r
    ALU, ACT, AX = mybir.AluOpType, mybir.ActivationFunctionType, mybir.AxisListType
    ds = bass.ds
    ctx = ExitStack()
    with ctx:
        here = [(nc.sbuf_base + 31) // 32 * 32]

        def at(name, shape, dt, offset=None):
            n = 4
            for s in shape[1:]:
                n *= s
            n = (n + 31) // 32 * 32
            o = here[0] if offset is None else offset
            if offset is None:
                here[0] += n
            return nc.alloc_sbuf_tensor_at(name, shape, dt, offset=o), o + n

        def sb(name, shape, dt=fp32):
            return at(name, shape, dt)[0]

        sems = {}

        def sem(name):
            sems[name] = ctx.enter_context(nc.semaphore(name))
            return sems[name]

        X = sb("X", [128, KB, T])
        RAW = sb("RAW", [128, 2, SLAB])
        WH = [sb(f"WH{n}", [128, SLAB], f32r) for n in range(2)]
        WL = [sb(f"WL{n}", [128, SLAB], f32r) for n in range(2)]
        PAR = sb("PAR", [128, NPAR])
        CST = sb("CST", [128, NCST, 128])
        ADA = sb("ADA", [128, NSUB, ADAM, 2])
        CT = sb("CT", [128, KB, 2])
        SC = sb("SC", [128, KB, 2])
        ACC = sb("ACC", [128, 2, 3, 2])
        EPS = sb("EPS", [128, 2])
        HH_AT = here[0]
        HH = sb("HH", [128, KB, T], f32r)
        HL_AT = here[0]
        HL = sb("HL", [128, KB, T], f32r)
        FREE = here[0]
        ident = CST[:, C_ID, :]

        def r32(n):
            return (n + 31) // 32 * 32

        def phase_memory(start, names):
            out, o = [], start
            for name, shape, dt in names:
                t, o = at(name, shape, dt, o)
                out.append(t)
            assert o <= nc.SBUF_PARTITION_SIZE_BYTES - 64, (names[0][0], o)
            return out

        TB, ADR, U0, U1, CV0, CV1, V0, V1, TAIL, PST = phase_memory(FREE, [
            ("TB", [128, KB, CW], fp32), ("ADR", [128, 6, SLAB], fp32),
            ("U0", [128, GAP + T], fp32), ("U1", [128, GAP + T], fp32),
            ("CV0", [128, T], fp32), ("CV1", [128, T], fp32),
            ("V0", [128, T], fp32), ("V1", [128, T], fp32),
            ("TAIL", [128, QKVB, 2, 3], fp32), ("PST", [128, 2, GPW], fp32)])
        CB, = phase_memory(FREE, [("CB", [128, 2, D], fp32)])
        AD0 = [phase_memory(o, [(f"AD0{n}", [128, KB, D], fp32)])[0] for n, o in enumerate((HH_AT, HL_AT, FREE))]
        UB, CV, VV = [U0, U1], [CV0, CV1], [V0, V1]
        AB_AT = (nc.SBUF_PARTITION_SIZE_BYTES - 64 - 4 * (T + 128 - DEC)) // 32 * 32
        AB, = phase_memory(AB_AT, [("AB", [128, T + 128 - DEC], fp32)])
        W8 = [128, HEADS, 128]
        OUTT, = phase_memory(HH_AT, [("OUTT", [128, KB, T], fp32)])
        (QKV, QN, KN, KBT, VB, KBE, KD, QE, KNT, QET, GAM, UU, TT, PP, WT, VN, SP0, SD, SS0, AQ, KQ,
         SSQ, RSQ, EXPO, GTT, SMS, AL, EE, EGL, BG, BETAG) = phase_memory(HL_AT, [
            ("QKV", [128, QKVB, 128], fp32)] + [(n, W8, fp32) for n in (
                "QN", "KN", "KBT", "VB", "KBE", "KD", "QE", "KNT", "QET", "GAM", "UU", "TT", "PP", "WT", "VN", "SP0", "SD", "SS0")]
            + [("AQ", [128, HEADS, 2, 128], fp32), ("KQ", [128, HEADS, 2, 128], fp32),
               ("SSQ", [128, 16], fp32), ("RSQ", [128, 16], fp32), ("EXPO", [128, 16], fp32), ("GTT", [128, 16], fp32),
               ("SMS", [128, 32], fp32), ("AL", [128, 8], fp32), ("EE", [128, 16], fp32), ("EGL", [128, 16], fp32), ("BG", [128, 8], fp32),
               ("BETAG", [128, GT + 1, 16], fp32)])
        KQ_AT = HL_AT + 4 * 128 * (QKVB + 18 * HEADS + 2 * HEADS)
        AM = phase_memory(KQ_AT, [("AM0", W8, fp32), ("AM1", W8, fp32)])
        SQ = phase_memory(HL_AT + 4 * 128 * (QKVB + 11 * HEADS), [("SQ0", W8, fp32), ("SQ1", W8, fp32)])
        GX, = phase_memory(HL_AT + 4 * 128 * QKVB, [("GX", [128, 4, GT + 1, HEADS], fp32)])

        ZL, SQC, OG, RS8, ROWS = phase_memory(FREE, [
            ("ZL", [128, 2, T], fp32), ("SQC", [128, 2, T], fp32), ("OG", [128, 2, T], fp32),
            ("RS8", [8, T], fp32), ("ROWS", [8, 8, 128], fp32)])
        LN_AT = FREE + 4 * KB * CW
        TB1, TB2, SQL0, SQL1, RST, SUMX = phase_memory(r32(LN_AT), [
            ("TB1", [128, KB, CW], fp32), ("TB2", [128, KB, CW], fp32), ("SQL0", [128, KB, CW], fp32), ("SQL1", [128, KB, CW], fp32),
            ("RST", [128, NCH, CW], fp32), ("SUMX", [128, T], fp32)])
        SQL = [SQL0, SQL1]
        (UF, CF, FT, FH, FL, PSF, TLF) = phase_memory(FREE, [
            ("UF", [128, 2, GAP + T], fp32), ("CF", [128, 2, T], fp32), ("FT", [128, T], fp32),
            ("FH", [128, 2, T], f32r), ("FL", [128, 2, T], f32r), ("PSF", [128, 2, FPW], fp32),
            ("TLF", [128, FB, 2, 2, 2], fp32)])
        LAT_AT = (LN_AT + 31) // 32 * 32 + 32
        CKH, CKL, KPE, QLH, QLL, COSN = phase_memory(LAT_AT, [
            ("CKH", [128, LB, KPAD], f32r), ("CKL", [128, LB, KPAD], f32r), ("KPE", [128, KEYS], fp32),
            ("QLH", [128, QB, T], f32r), ("QLL", [128, QB, T], f32r), ("COSN", [128, 2, T], fp32)])
        CKF, = phase_memory(LAT_AT + 4 * LB * KPAD, [("CKF", [128, LB, KPAD], fp32)])
        QLF, = phase_memory(LAT_AT + 8 * LB * KPAD + r32(4 * KEYS) + r32(4 * QB * T), [("QLF", [128, QB, T], fp32)])
        QPE, QT, KT, VT, PR0, PR1, PT, OH0, OH1, SMX, MSK, QPC = phase_memory(HH_AT, [
            ("QPE", [128, HEADS // 2, T], fp32), ("QT", [128, T], fp32), ("KT", [128, KEYS], fp32), ("VT", [128, 11, 128], fp32),
            ("PR0", [128, SEQ], fp32), ("PR1", [128, SEQ], fp32), ("PT", [128, 8, 128], fp32),
            ("OH0", [128, T], fp32), ("OH1", [128, T], fp32), ("SMX", [128, 4, GT + 1], fp32), ("MSK", [1, 2, 128], fp32), ("QPC", [128, T], fp32)])
        PR, OH = [PR0, PR1], [OH0, OH1]
        OL = phase_memory(FREE, [(f"OL{n}", [128, KB, CW], fp32) for n in range(NCH)])
        SQM, RSM = phase_memory(FREE, [("SQM", [128, 2, 3, CW], fp32), ("RSM", [128, 2, CW], fp32)])

        PS = ctx.enter_context(nc.psum_tensor("PS", [128, 8, 512], fp32))
        B_ADA = 6

        scr = nc.dram_tensor("scr", (QKVB + ZB, 128, T), fp32, kind="Internal").ap()

        x_ld, par_ld, c_ld = sem("x_ld"), sem("par_ld"), sem("c_ld")
        raw_ld = [sem(f"raw_ld{n}") for n in range(2)]
        hi_done, lo_done = sem("hi_done"), sem("lo_done")
        ws_begun = sem("ws_begun")
        ada0_ld = [sem(f"ada0_ld{n}") for n in range(3)]
        ada_ld = [sem(f"ada_ld{n}") for n in range(6)]
        ada0_ps, cb_ld, cb_rdy, ada_ch, ada_sum = sem("ada0_ps"), sem("cb_ld"), sem("cb_rdy"), sem("ada_ch"), sem("ada_sum")
        ada_used = sem("ada_used")
        sc_done = sem("sc_done")
        ada_done = sem("ada_done")
        x_scaled = sem("x_scaled")
        tmp_rdy, hh_rdy, hl_rdy = sem("tmp_rdy"), sem("hh_rdy"), sem("hl_rdy")
        vec_ch, act_ch, pool_ch = sem("vec_ch"), sem("act_ch"), sem("pool_ch")
        ini = sem("ini")
        out_done, y_st = sem("out_done"), sem("y_st")
        up_done, up_ev = sem("up_done"), sem("up_ev")
        pst_rdy, conv_done, v_done, v_st = sem("pst_rdy"), sem("conv_done"), sem("v_done"), [sem("v_st0"), sem("v_st1")]
        tail_rdy = sem("tail_rdy")
        pool_step, pe_step = sem("pool_step"), sem("pe_step")
        z_ld = [sem("z_ld0"), sem("z_ld1")]
        sqc_rdy, ss_ps, rs_rdy, rb_ps, og_rdy, oh_rdy, ol_rdy, rb_ev = (sem(n) for n in (
            "sqc_rdy", "ss_ps", "rs_rdy", "rb_ps", "og_rdy", "oh_rdy", "ol_rdy", "rb_ev"))
        ln_g, sum_rdy, mean_ps, cen_rdy, lsq_rdy, var_ps, std_rdy, nrl_rdy, x_rdy = (sem(n) for n in (
            "ln_g", "sum_rdy", "mean_ps", "cen_rdy", "lsq_rdy", "var_ps", "std_rdy", "nrl_rdy", "x_rdy"))
        psf_rdy, uf_ev, cf_ch, cf_rdy, sil_rdy, ft_rdy, fh_rdy, fl_rdy, dn_ps, dn_ev, tlf_rdy = (sem(n) for n in (
            "psf_rdy", "uf_ev", "cf_ch", "cf_rdy", "sil_rdy", "ft_rdy", "fh_rdy", "fl_rdy", "dn_ps", "dn_ev", "tlf_rdy"))
        (kv_ld, pad_rdy, msq_rdy, msum_ps, mstd_rdy, mrc_rdy, mnrm_rdy, rot_ps, rot_ev, rot_ch, rope_rdy, lh_rdy, ll_rdy) = (sem(n) for n in (
            "kv_ld", "pad_rdy", "msq_rdy", "msum_ps", "mstd_rdy", "mrc_rdy", "mnrm_rdy", "rot_ps", "rot_ev", "rot_ch", "rope_rdy", "lh_rdy", "ll_rdy"))
        (pj_ps, qv_ev, k_ev, qc_rdy, sc_ps, mx_rdy, ex_rdy, nm_rdy, pt_ps, pt_ev, pu_ps, pu_ev, ov_ps, ov_ev) = (sem(n) for n in (
            "pj_ps", "qv_ev", "k_ev", "qc_rdy", "sc_ps", "mx_rdy", "ex_rdy", "nm_rdy", "pt_ps", "pt_ev", "pu_ps", "pu_ev", "ov_ps", "ov_ev"))
        o_st, o_ld = [sem("o_st0"), sem("o_st1")], [sem(f"o_ld{n}") for n in range(NCH)]
        ab_rdy, ab_ps, gx, bg_rdy = sem("ab_rdy"), sem("ab_ps"), sem("gx"), sem("bg_rdy")
        qkv_ld, gtt_rdy, gbc_rdy, sm_ps, sms_rdy = sem("qkv_ld"), sem("gtt_rdy"), sem("gbc_rdy"), sem("sm_ps"), sem("sms_rdy")
        t1_ps, sq_rdy, ssq_rdy, rsq_rdy, nrm_rdy = sem("t1_ps"), sem("sq_rdy"), sem("ssq_rdy"), sem("rsq_rdy"), sem("nrm_rdy")
        ee_rdy, bgg_rdy, mix_rdy, gb_ps, gam_rdy = sem("ee_rdy"), sem("bgg_rdy"), sem("mix_rdy"), sem("gb_ps"), sem("gam_rdy")
        t2_ps, knt_rdy, kq_rdy, qet_rdy = sem("t2_ps"), sem("knt_rdy"), sem("kq_rdy"), sem("qet_rdy")
        kk_ps, aq_rdy, am_rdy, u_rdy, t_rdy = sem("kk_ps"), sem("aq_rdy"), sem("am_rdy"), sem("u_rdy"), sem("t_rdy")
        tu_ps, pp_ps, pp_rdy, tn_ps, un_ps = sem("tu_ps"), sem("pp_ps"), sem("pp_rdy"), sem("tn_ps"), sem("un_ps")
        wt_ps, wt_rdy, vn_ps, vn_rdy, sn_ps, oo_ps = sem("wt_ps"), sem("wt_rdy"), sem("vn_ps"), sem("vn_rdy"), sem("sn_ps"), sem("oo_ps")
        oo_rdy, sd_rdy, s_rdy, s0_ld, g_ini, rs_ch = sem("oo_rdy"), sem("sd_rdy"), sem("s_rdy"), sem("s0_ld"), sem("g_ini"), sem("rs_ch")

        def need(e, s, count):
            e.wait_ge(s, count + CREDIT.get(s, 0))
            if not isinstance(count, int) and e.engine == mybir.EngineType.Pool:
                e.sem_inc(pool_step, 1)

        CREDIT = {ada_used: 4, up_ev: 6, conv_done: 2, tail_rdy: 2, v_st[0]: 16, v_st[1]: 16, v_done: 2, dn_ev: 2,
                  gam_rdy: 1, wt_rdy: 1, oo_rdy: 1, s_rdy: 1, sm_ps: 1, ee_rdy: 1, kk_ps: 1,
                  ex_rdy: 1, pt_ev: 1, pu_ev: 1, ov_ev: 1, sc_ps: 1, pu_ps: 1, o_st[0]: 16, o_st[1]: 16}

        def split_hi(e, n, u):
            need(e, raw_ld[u], (n - u) * 8 + 16)
            need(e, ws_begun, n)
            e.activation(WH[u][:, :], RAW[:, u, :], ACT.Copy).then_inc(hi_done, 1)

        def split_lo(e, n, u):
            need(e, hi_done, n + 1)
            e.tensor_tensor(WL[u][:, :], RAW[:, u, :], WH[u][:, :].bitcast(fp32), ALU.subtract).then_inc(lo_done, 1)

        def three(e, out, w, c, mh, ml, first, last, begins=False):
            mm = e.matmul(out, WH[w][:, c:c + 128], mh, start=first, stop=False)
            if begins:
                mm.then_inc(ws_begun, 1)
            e.matmul(out, WH[w][:, c:c + 128], ml, start=False, stop=False)
            return e.matmul(out, WL[w][:, c:c + 128], mh, start=False, stop=last)

        def dense(e, n, u, g, gu, ready=None, kb=KB, mh=None, ml=None, c=0, begins=True):
            need(e, hi_done, n + 1)
            need(e, lo_done, n + 1)
            for ch, (c0, cw) in enumerate(CHS):
                if ready:
                    ready(ch)
                need(e, up_ev, 3 * (g - 2) + ch + 1)
                for k in range(kb):
                    mm = three(e, PS[:, 3 * gu + ch, 0:cw], u, c + k * 128, (mh or HH)[:, k, c0:c0 + cw],
                               (ml or HL)[:, k, c0:c0 + cw], k == 0, k == kb - 1, begins and ch == 0 and k == 0)
                mm.then_inc(up_done, 1)

        def hin_ready(e, hs):
            def ready(ch):
                need(e, hh_rdy, 3 * hs + ch + 1)
                need(e, hl_rdy, 3 * hs + ch + 1)
            return ready

        def all_of(e, *pairs):
            def ready(ch):
                for s_, n_ in pairs:
                    need(e, s_, n_)
            return ready

        PRO, SAMP = (0, SAM), (SAM, T)

        def pieces(c0, cw):
            out = []
            for st, (a, b) in enumerate((PRO, SAMP)):
                lo, hi = max(a, c0), min(b, c0 + cw)
                if lo < hi:
                    out.append((lo, hi - lo, st))
            return out

        def pe_ada(e):
            for t in range(3):
                e.wait_ge(ada0_ld[t], 16)
                for m in range(KB):
                    for k in range(KB):
                        mm = e.matmul(PS[:, B_ADA, 2 * (KB * t + m):2 * (KB * t + m) + 2], AD0[t][:, m, k * 128:(k + 1) * 128], SC[:, k, :],
                                      start=(k == 0), stop=(k == KB - 1))
            mm.then_inc(ada0_ps, 1)

        def vec_ada(v):
            v.wait_ge(ada0_ps, 1)
            b = PAR[:, P_ADAB:P_ADAB + ADAM].unsqueeze(2).to_broadcast([128, ADAM, 2])
            v.tensor_tensor(ADA[:, 0, :, :], PS[:, B_ADA, 0:2 * ADAM].rearrange("p (m c) -> p m c", c=2), b, ALU.add).then_inc(ada_done, 1)
            v.wait_ge(ada_done, 1)
            vec_ada_constants(v, 0, 1)
            v.wait_ge(ada_done, 3)

        def vec_ada_constants(v, s, e):
            v.tensor_scalar(ADA[:, s:e, KB:2 * KB, :], ADA[:, s:e, KB:2 * KB, :], 1.0, 1.0 / ALPHA, ALU.add, ALU.mult).then_inc(ada_done, 1)
            v.tensor_scalar(ADA[:, s:e, 2 * KB:, :], ADA[:, s:e, 2 * KB:, :], 1.0, None, ALU.add).then_inc(ada_done, 1)

        def ada_of(n, z):
            return (3 * n - QKVB, 3) if z else (2 * n, 2)

        def load_ada(e, n, u, z):
            m, k = ada_of(n, z)
            for q in range(k):
                need(e, ada_used, m - 2 if z else 2 * (n - 2) + q + 1)
                e.dma_start(ADR[:, 3 * u + q, :], wada[ds(m + q, 1), :, :].rearrange("a p n -> p (a n)")).then_inc(ada_ld[3 * u + q], 16)

        def vec_ada_sums(v, n, u, i, z):
            m, k = ada_of(n, z)
            for q in range(k):
                need(v, ada_ld[3 * u + q], 16 * (i - QKVB // 2) + 16 if q == 2 else 16 * i + 16)
                need(v, cb_rdy, 1)
                for st in range(2):
                    if st:
                        need(v, ada_ch, m + q + 1)
                    else:
                        need(v, ada_used, m + q)
                    ins = v.tensor_tensor_reduce(out=PS[:, B_ADA:B_ADA + 2, :].rearrange("p b c -> p (b c)"), in0=ADR[:, 3 * u + q, :], in1=CB[:, st, :],
                                                 scale=1.0, scalar=0.0, op0=ALU.mult, op1=ALU.add, accum_out=ACC[:, u, q, st:st + 1])
                    ins.then_inc(ada_used if st else ada_ch, 1)
            need(v, ada_used, m + k)
            v.tensor_tensor(ADA[:, :, :, :].rearrange("p s m c -> p (s m) c")[:, ds(m + ADAM, k), :], ACC[:, u, 0:k, :],
                            PAR[:, ds(m + P_ADAB + ADAM, k)].unsqueeze(2).to_broadcast([128, k, 2]), ALU.add).then_inc(ada_sum, 1)

        def tb(hs, ch):
            return TB if hs == 3 else (TB, TB1, TB2)[ch]

        def made(hs, ch):
            return 3 * (hs - (hs > 4)) + ch + 1

        def act_hin_chunk(a, hs):
            def hin(ch):
                c0, cw = CHS[ch]
                a.wait_ge(tmp_rdy, made(hs, ch))
                a.activation(HH[:, :, c0:c0 + cw], tb(hs, ch)[:, :, 0:cw], ACT.Copy).then_inc(hh_rdy, 1)
            return hin

        def make_hin(e, s, hs, ch):
            c0, cw = CHS[ch]
            out = tb(hs, ch)
            if s is None:
                ins = e.tensor_scalar(out[:, :, 0:cw], X[:, :, c0:c0 + cw], 1.0 / ALPHA, None, ALU.mult)
            else:
                for b in range(KB):
                    for a, w, st in pieces(c0, cw):
                        ins = e.tensor_scalar(out[:, b, a - c0:a - c0 + w], X[:, b, a:a + w], ADA[:, s, KB + b, st:st + 1],
                                              ADA[:, s, b, st:st + 1], ALU.mult, ALU.add)
            ins.then_inc(tmp_rdy, 1)

        def vec_lower(v, hs, ch):
            c0, cw = CHS[ch]
            v.wait_ge(hh_rdy, 3 * hs + ch + 1)
            v.wait_ge(tmp_rdy, made(hs, ch))
            v.tensor_tensor(HL[:, :, c0:c0 + cw], tb(hs, ch)[:, :, 0:cw], HH[:, :, c0:c0 + cw].bitcast(fp32),
                            ALU.subtract).then_inc(hl_rdy, 1)

        def vec_hin_chunk(v, s, hs):
            def hin(ch):
                if hs == 3 and ch:
                    v.wait_ge(hl_rdy, 3 * hs + ch)
                make_hin(v, s, hs, ch)
                vec_lower(v, hs, ch)
            return hin

        def every(hin):
            for ch in range(NCH):
                hin(ch)

        def hist_cols(u):
            w = GAP + DEC
            return UB[u][:, SEQ + GAP - w:GAP + T].rearrange("p (s c) -> p s c", s=2)[:, :, w - (GC - 1):]

        NL = len(LEVELS)
        PROMPT_TILE = (128, CHUNK, 128 // CHUNK, NL)
        SAMPLE_TILE = (DEC, DEC, 1, NL - 1)
        G2 = range(2)

        def con(m, P=128, M=128):
            return CST[0:P, m, 0:M]

        def grp(t, g, P=128):
            return t[0:P, 4 * g:4 * g + 4, :]

        def bank(b, P=128, M=128):
            return PS[0:P, b, :].rearrange("p (h c) -> p h c", h=4)[:, :, 0:M]

        def two(b, P=128):
            return PS[0:P, b:b + 2, :].rearrange("p b (h c) -> p (b h) c", h=4)

        def per_head(t, P, c, n=HEADS):
            return t[0:P, c:c + n].unsqueeze(2).to_broadcast([P, n, 128])

        def tile_start(i):
            return 128 * i if not isinstance(i, int) or i < GT else SAM

        def load_qkv(a, i, P):
            need(a, t1_ps, 6 * i)
            for m in range(3):
                a.dma_start(QKV[:, 8 * m:8 * m + 8, 0:P],
                             scr[8 * m:8 * m + 8, :, ds(tile_start(i), P)].rearrange("b p t -> p b t")).then_inc(qkv_ld, 16)

        def pe_g(e, i, tile, S):
            P, C, nch, nl = tile
            need(e, gtt_rdy, i + 1)
            need(e, gam_rdy, 8 * i)
            need(e, wt_rdy, 2 * i)
            e.matmul(PS[0:P, 6, 0:8], con(C_CUM, P, P), GTT[0:P, 0:8], start=True, stop=True)
            for c in range(nch):
                e.matmul(PS[:, 6, 8 + 8 * c:16 + 8 * c], con(C_IND0 + c, P), GTT[0:P, 0:8], start=True, stop=True)
            e.matmul(PS[0:P, 6, 24:32], con(C_SAME, P, P), GTT[0:P, 0:8], start=True, stop=True).then_inc(sm_ps, 1)
            need(e, qkv_ld, 48 * i + 48)
            need(e, oo_rdy, 2 * i)
            need(e, s_rdy, 4 * i)
            for m in range(3):
                for g in G2:
                    for h in range(4):
                        mm = e.transpose(PS[0:P, 2 * m + g, h * 128:(h + 1) * 128], QKV[:, 8 * m + 4 * g + h, 0:P], ident)
                    mm.then_inc(t1_ps, 1)
            need(e, gbc_rdy, i + 1)
            need(e, sms_rdy, 2 * i + 1)
            for g in G2:
                for h in range(4):
                    out = PS[0:P, 6 + g, h * 128:h * 128 + P]
                    e.matmul(out, KNT[0:P, 4 * g + h, 0:P], con(C_CUM, P, P), start=True, stop=False)
                    mm = e.matmul(out, con(C_ID, P, P), con(C_NEG, P, P), start=False, stop=True)
                mm.then_inc(gb_ps, 1)
            for m, (src, rdy, n) in enumerate(((KN, nrm_rdy, 3), (QN, nrm_rdy, 3), (KBT, mix_rdy, 1), (QE, mix_rdy, 2))):
                need(e, rdy, (3 if rdy is nrm_rdy else 4) * i + n)
                if m == 3:
                    need(e, gam_rdy, 8 * i + 8)
                for g in G2:
                    for h in range(4):
                        mm = e.transpose(PS[:, 2 * m + g, h * 128:h * 128 + P], src[0:P, 4 * g + h, :], con(C_ID, P, P))
                    mm.then_inc(t2_ps, 1)
            need(e, knt_rdy, 2 * i + 2)
            need(e, kq_rdy, 4 * i + 4)
            for b in range(4):
                for hh in range(2):
                    h = 2 * b + hh
                    mm = e.matmul(PS[0:P, b, hh * 256:hh * 256 + 2 * P], KNT[:, h, 0:P], KQ[:, h, :, 0:P], start=True, stop=True)
                mm.then_inc(kk_ps, 1)
            need(e, u_rdy, 12 * i + 2)
            for g in G2:
                for h in range(4):
                    mm = e.transpose(PS[0:P, 4 + g, h * 128:h * 128 + P], UU[0:P, 4 * g + h, 0:P], con(C_ID, P, P))
                mm.then_inc(tu_ps, 1)

            def prod(b, g, a, c, s):
                for h in range(4 * g, 4 * g + 4):
                    mm = e.matmul(PS[0:P, b + g, (h % 4) * 128:(h % 4) * 128 + P], a[0:P, h, 0:P], c[0:P, h, 0:P], start=True, stop=True)
                mm.then_inc(s, 1)
            for n in range(nl):
                need(e, am_rdy, 6 * i + n + 2)
                for g in G2:
                    need(e, t_rdy, 10 * i + 2 * n + g + 1)
                    need(e, u_rdy, 12 * i + 2 * n + g + 1)
                    need(e, aq_rdy, 4 * i + 4)
                    prod(0, g, AM[(n + 1) % 2], TT, pp_ps)
                for g in G2:
                    need(e, pp_rdy, 10 * i + 2 * n + g + 1)
                    if n < nl - 1:
                        prod(2, g, UU, PP, tn_ps)
                    prod(4, g, PP, UU, un_ps)
            need(e, qet_rdy, 2 * i + 2)
            for g in G2:
                need(e, u_rdy, 12 * i + 2 * nl + g + 1)
                for h in range(4 * g, 4 * g + 4):
                    mm = e.matmul(PS[:, 6 + g, (h % 4) * 128:(h % 4) * 128 + P], KBE[0:P, h, :], UU[0:P, h, 0:P], start=True, stop=True)
                mm.then_inc(wt_ps, 1)
            for c in range(nch):
                r0, r1 = c * C, c * C + C
                for g in G2:
                    need(e, wt_rdy, 2 * i + g + 1)
                    need(e, s_rdy, 4 * i + 2 * c)
                    if c:
                        need(e, vn_rdy, 4 * i + 2 * c)
                    for h in range(4 * g, 4 * g + 4):
                        out = PS[r0:r1, g, (h % 4) * 128:(h % 4) * 128 + 128]
                        e.matmul(out, UU[0:P, h, r0:r1], VB[0:P, h, :], start=True, stop=False)
                        mm = e.matmul(out, WT[:, h, r0:r1], S[:, h, :], start=False, stop=True)
                    mm.then_inc(vn_ps, 1)
                if c:
                    need(e, oo_rdy, 2 * i + c)
                for g in G2:
                    need(e, vn_rdy, 4 * i + 2 * c + g + 1)
                    for h in range(4 * g, 4 * g + 4):
                        mm = e.matmul(PS[:, 4 + g, (h % 4) * 128:(h % 4) * 128 + 128], KD[r0:r1, h, :], VN[r0:r1, h, :], start=True, stop=True)
                    mm.then_inc(sn_ps, 1)
                    for h in range(4 * g, 4 * g + 4):
                        out = PS[:, 2, h * CHUNK:h * CHUNK + C]
                        e.matmul(out, S[:, h, :], QET[:, h, r0:r1], start=True, stop=False)
                        mm = e.matmul(out, VN[r0:r1, h, :], AQ[r0:r1, h, 1, r0:r1], start=False, stop=True)
                    mm.then_inc(oo_ps, 1)

        def act_g(a, i, tile, P_next):
            P, C, nch, nl = tile
            for m in G2:
                need(a, t1_ps, 6 * i + 2 * m + 2)
                a.activation(SQ[m][0:P, :, :], two(2 * m, P), ACT.Square).then_inc(sq_rdy, 1)
            if P_next:
                load_qkv(a, i + 1, P_next)
            need(a, sms_rdy, 2 * i + 2)
            a.activation(EE[0:P, :], SMS[0:P, 0:16], ACT.Exp)
            a.activation(EGL[:, 0:8 * nch], SMS[:, 16:16 + 8 * nch], ACT.Exp).then_inc(ee_rdy, 1)
            for h in range(HEADS):
                if h % 4 == 0:
                    need(a, gb_ps, 2 * i + h // 4 + 1)
                a.activation(GAM[0:P, h, 0:P], PS[0:P, 6 + h // 4, (h % 4) * 128:(h % 4) * 128 + P], ACT.Exp,
                             bias=GTT[0:P, 8 + h:9 + h]).then_inc(gam_rdy, 1)
            for g in G2:
                need(a, t2_ps, 8 * i + g + 1)
                a.activation(grp(KNT, g)[:, :, 0:P], bank(g, 128, P), ACT.Copy).then_inc(knt_rdy, 1)
            for g in G2:
                need(a, t2_ps, 8 * i + 6 + g + 1)
                a.activation(grp(QET, g)[:, :, 0:P], bank(6 + g, 128, P), ACT.Copy).then_inc(qet_rdy, 1)
            for g in G2:
                need(a, tu_ps, 2 * i + g + 1)
                a.activation(grp(TT, g, P)[:, :, 0:P], bank(4 + g, P, P), ACT.Copy).then_inc(t_rdy, 1)
            for n in range(nl):
                for g in G2:
                    need(a, pp_ps, 10 * i + 2 * n + g + 1)
                    a.activation(grp(PP, g, P)[:, :, 0:P], bank(g, P, P), ACT.Copy).then_inc(pp_rdy, 1)
            for g in G2:
                need(a, wt_ps, 2 * i + g + 1)
                a.activation(grp(WT, g)[:, :, 0:P], bank(6 + g, 128, P), ACT.Copy, scale=-1.0).then_inc(wt_rdy, 1)
            for c in range(nch):
                r0, r1 = c * C, c * C + C
                for g in G2:
                    need(a, vn_ps, 4 * i + 2 * c + g + 1)
                    a.activation(VN[r0:r1, 4 * g:4 * g + 4, :], PS[r0:r1, g, :].rearrange("p (h c) -> p h c", h=4), ACT.Copy).then_inc(vn_rdy, 1)
                need(a, oo_ps, 4 * i + 2 * c + 2)
                a.activation(OUTT[:, :, ds(tile_start(i) + r0, C)],
                             PS[:, 2, :].rearrange("p (h c) -> p h c", h=8)[:, :, 0:C], ACT.Copy).then_inc(oo_rdy, 1)

        def vec_g(v, i, tile, S):
            P, C, nch, nl = tile
            need(v, sm_ps, i)
            need(v, gam_rdy, 8 * i)
            v.tensor_copy(GTT[:, :], BETAG[:, ds(i, 1), :].rearrange("p a c -> p (a c)")).then_inc(gtt_rdy, 1)
            need(v, sm_ps, i + 1)
            need(v, ee_rdy, i)
            need(v, gtt_rdy, i + 1)
            v.tensor_copy(SMS[0:P, 0:8], PS[0:P, 6, 0:8])
            v.tensor_copy(SMS[:, 16:16 + 8 * nch], PS[:, 6, 8:8 + 8 * nch])
            v.tensor_copy(SMS[0:P, 8:16], PS[0:P, 6, 24:32]).then_inc(sms_rdy, 1)
            v.wait_ge(sms_rdy, 2 * i + 1)
            v.tensor_scalar(GTT[0:P, 8:16], SMS[0:P, 0:8], -1.0, None, ALU.mult)
            v.tensor_tensor(SMS[0:P, 8:16], SMS[0:P, 8:16], SMS[0:P, 0:8], ALU.subtract).then_inc(sms_rdy, 1)
            for m in G2:
                need(v, sq_rdy, 2 * i + m + 1)
                v.tensor_reduce(SSQ[0:P, 8 * m:8 * m + 8], SQ[m][0:P, :, :], AX.X, ALU.add).then_inc(ssq_rdy, 1)
            need(v, rsq_rdy, 2 * i + 2)
            for dst, b, c in ((KN, 2, 8), (QN, 0, 0), (VB, 4, None)):
                sc = BETAG[0:P, ds(i, 1), 8:16].rearrange("p a c -> p (a c)").unsqueeze(2).to_broadcast([P, 8, 128]) if c is None else per_head(RSQ, P, c)
                if c is None:
                    need(v, t1_ps, 6 * i + 6)
                v.tensor_tensor(dst[0:P, :, :], two(b, P), sc, ALU.mult).then_inc(nrm_rdy, 1)
            for m in (1, 0):
                for g in G2:
                    b = 2 if m else 4
                    need(v, t2_ps, 8 * i + b + g + 1)
                    v.tensor_copy(KQ[:, 4 * g:4 * g + 4, m, 0:P], bank(b + g, 128, P)).then_inc(kq_rdy, 1)
            need(v, gam_rdy, 8 * i + 8)
            for b in range(4):
                need(v, kk_ps, 4 * i + b + 1)
                v.tensor_tensor(AQ[0:P, 2 * b:2 * b + 2, :, 0:P],
                                PS[0:P, b, :].rearrange("p (h c) -> p h c", h=2)[:, :, 0:2 * P].rearrange("p h (x c) -> p h x c", x=2),
                                GAM[0:P, 2 * b:2 * b + 2, 0:P].unsqueeze(2).to_broadcast([P, 2, 2, P]), ALU.mult).then_inc(aq_rdy, 1)
            need(v, am_rdy, 6 * i + 1)
            for g in G2:
                v.tensor_tensor(grp(UU, g, P)[:, :, 0:P], con(C_ID, P, P).unsqueeze(1).to_broadcast([P, 4, P]),
                                grp(AM[0], g, P)[:, :, 0:P], ALU.subtract).then_inc(u_rdy, 1)
            for n in range(nl):
                for g in G2:
                    if n < nl - 1:
                        need(v, tn_ps, 8 * i + 2 * n + g + 1)
                        need(v, t_rdy, 10 * i + 2 * n + g + 1)
                        v.tensor_tensor(grp(TT, g, P)[:, :, 0:P], grp(TT, g, P)[:, :, 0:P], bank(2 + g, P, P), ALU.subtract).then_inc(t_rdy, 1)
                    need(v, un_ps, 10 * i + 2 * n + g + 1)
                    need(v, u_rdy, 12 * i + 2 * n + g + 1)
                    v.tensor_tensor(grp(UU, g, P)[:, :, 0:P], grp(UU, g, P)[:, :, 0:P], bank(4 + g, P, P), ALU.subtract).then_inc(u_rdy, 1)
            for c in range(nch):
                for g in G2:
                    need(v, oo_ps, 4 * i + 2 * c + g + 1)
                    need(v, sd_rdy, 4 * i + 2 * c + g + 1)
                    v.tensor_tensor(grp(S, g), grp(SD, g), PS[:, 4 + g, :].rearrange("p (h c) -> p h c", h=4), ALU.add).then_inc(s_rdy, 1)

        def pool_g(p, i, tile, S):
            P, C, nch, nl = tile
            need(p, gtt_rdy, i + 1)
            need(p, kk_ps, 4 * i)
            p.tensor_copy(KNT[0:P, :, 0:P], GTT[0:P, 0:8].unsqueeze(2).to_broadcast([P, 8, P])).then_inc(gbc_rdy, 1)
            need(p, ssq_rdy, 2 * i + 2)
            p.tensor_scalar(SSQ[0:P, :], SSQ[0:P, :], RMS_EPS, None, ALU.add).then_inc(rs_ch, 1)
            need(p, rs_ch, 2 * i + 1)
            p.tensor_tensor(RSQ[0:P, :], SSQ[0:P, :], EXPO[0:P, :], ALU.pow).then_inc(rs_ch, 1)
            need(p, rs_ch, 2 * i + 2)
            p.tensor_scalar(RSQ[0:P, 0:8], RSQ[0:P, 0:8], 128 ** -0.5, None, ALU.mult).then_inc(rsq_rdy, 1)
            need(p, ee_rdy, i + 1)
            p.tensor_tensor(BG[0:P, :], BETAG[0:P, ds(i, 1), 8:16].rearrange("p a c -> p (a c)"), EE[0:P, 0:8], ALU.mult).then_inc(rsq_rdy, 1)
            need(p, nrm_rdy, 3 * i + 3)
            need(p, rsq_rdy, 2 * i + 2)
            beta = BETAG[0:P, ds(i, 1), 8:16].rearrange("p a c -> p (a c)").unsqueeze(2).to_broadcast([P, 8, 128])
            for dst, src, sc in ((KBT, KN, beta), (QE, QN, per_head(EE, P, 0)), (KBE, KN, per_head(BG, P, 0)), (KD, KN, per_head(EE, P, 8))):
                p.tensor_tensor(dst[0:P, :, :], src[0:P, :, :], sc, ALU.mult).then_inc(mix_rdy, 1)
            need(p, aq_rdy, 4 * i + 4)
            for n in range(nl + 1):
                if n >= 2:
                    need(p, pp_ps, 10 * i + 2 * (n - 1))
                p.tensor_tensor(AM[n % 2][0:P, :, 0:P], AQ[0:P, :, 0, 0:P],
                                con(C_MASK + n, P, P).unsqueeze(1).to_broadcast([P, 8, P]), ALU.mult).then_inc(am_rdy, 1)
            for c in range(nch):
                for g in G2:
                    need(p, s_rdy, 4 * i + 2 * c)
                    p.tensor_tensor(grp(SD, g), grp(S, g), EGL[:, 8 * c + 4 * g:8 * c + 4 * g + 4].unsqueeze(2).to_broadcast([128, 4, 128]),
                                    ALU.mult).then_inc(sd_rdy, 1)

        G_WO = QKVB + ZB + 1
        OUTS_G = 48

        def act_gate(a):
            a.wait_ge(out_done, OUTS_G)
            a.dma_start(ROWS[:, :, :], rows).then_inc(c_ld, 16)
            for h in range(HEADS):
                if h >= 2:
                    a.wait_ge(ss_ps, h - 1)
                if h == 0:
                    need(a, oo_rdy, 2 * GT + 1)
                a.activation(SQC[:, h % 2, :], OUTT[:, h, :], ACT.Square).then_inc(sqc_rdy, 1)
            a.wait_ge(ss_ps, HEADS)
            for ch, (c0, cw) in enumerate(CHS):
                ins = a.activation(RS8[:, c0:c0 + cw], PS[0:8, ch, 0:cw], ACT.Sqrt, scale=1.0 / 128, bias=EPS[0:8, 1:2])
            ins.then_inc(sqc_rdy, 1)
            for h in range(HEADS):
                if h >= 2:
                    a.wait_ge(og_rdy, h - 1)
                a.dma_start(ZL[:, h % 2, :], scr[QKVB + h, :, :]).then_inc(z_ld[h % 2], 16)
                if h:
                    a.wait_ge(og_rdy, h)
                    a.wait_ge(rb_ev, 3 * h + 1)
                    a.activation(HH[:, h - 1, :], OG[:, (h - 1) % 2, :], ACT.Copy).then_inc(oh_rdy, 1)
            a.wait_ge(og_rdy, HEADS)
            a.activation(HH[:, HEADS - 1, :], OG[:, (HEADS - 1) % 2, :], ACT.Copy).then_inc(oh_rdy, 1)

        def pe_gate(e):
            for h in range(HEADS):
                e.wait_ge(sqc_rdy, h + 1)
                for ch, (c0, cw) in enumerate(CHS):
                    mm = e.matmul(PS[0:8, ch, 0:cw], con(C_SELC)[:, 8 * h:8 * h + 8], SQC[:, h % 2, c0:c0 + cw],
                                  start=(h == 0), stop=(h == HEADS - 1))
                mm.then_inc(ss_ps, 1)
            e.wait_ge(rs_rdy, 1)
            e.wait_ge(c_ld, 32)
            for h in range(HEADS):
                for ch, (c0, cw) in enumerate(CHS):
                    if 3 * h + ch >= 5:
                        e.wait_ge(rb_ev, 3 * h + ch - 4)
                    e.matmul(PS[:, 3 + (3 * h + ch) % 5, 0:cw], ROWS[:, h, :], RS8[:, c0:c0 + cw], start=True, stop=True).then_inc(rb_ps, 1)

        def vec_gate(v):
            v.wait_ge(sqc_rdy, HEADS + 1)
            v.reciprocal(RS8[:, :], RS8[:, :]).then_inc(rs_rdy, 1)
            for h in range(HEADS):
                if h >= 2:
                    v.wait_ge(oh_rdy, h - 1)
                    v.wait_ge(ol_rdy, h - 1)
                for ch, (c0, cw) in enumerate(CHS):
                    v.wait_ge(rb_ps, 3 * h + ch + 1)
                    v.tensor_tensor(OG[:, h % 2, c0:c0 + cw], OUTT[:, h, c0:c0 + cw], PS[:, 3 + (3 * h + ch) % 5, 0:cw], ALU.mult).then_inc(rb_ev, 1)
                v.wait_ge(rb_ev, 3 * h + 3)
                v.wait_ge(z_ld[h % 2], 16 * (h // 2) + 16)
                v.scalar_tensor_tensor(OG[:, h % 2, :], OG[:, h % 2, :], PAR[:, P_GNG:P_GNG + 1], ZL[:, h % 2, :],
                                       ALU.mult, ALU.mult).then_inc(og_rdy, 1)

        def pool_gate(p):
            for h in range(HEADS):
                p.wait_ge(oh_rdy, h + 1)
                p.tensor_tensor(HL[:, h, :], OG[:, h % 2, :], HH[:, h, :].bitcast(fp32), ALU.subtract).then_inc(ol_rdy, 1)

        def act_split_run(a, n0, n):
            for q in range(n):
                split_hi(a, n0 + q, (n0 + q) % 2)

        def pool_split_run(p, n0, n):
            for q in range(n):
                split_lo(p, n0 + q, (n0 + q) % 2)

        def pe_proj(e, n0, g0, ready):
            for m in range(KB):
                dense(e, n0 + m, (n0 + m) % 2, g0 + m, (g0 + m) % 2, ready if m == 0 else None)

        def vec_proj(v, s, g0):
            for m in range(KB):
                for ch, (c0, cw) in enumerate(CHS):
                    need(v, up_done, 3 * (g0 + m) + ch + 1)
                    for a, w, st in pieces(c0, cw):
                        ins = v.scalar_tensor_tensor(X[:, m, a:a + w], PS[:, 3 * ((g0 + m) % 2) + ch, a - c0:a - c0 + w],
                                                     ADA[:, s, 2 * KB + m, st:st + 1], X[:, m, a:a + w], ALU.mult, ALU.add)
                    ins.then_inc(up_ev, 1)

        def mixed_up(g0):
            return lambda e, m, ch: need(e, up_ev, 3 * (g0 + m) + ch + 1)

        def mixed_down(l):
            return lambda e, m, ch: need(e, dn_ev, (l + 1) * 3 * KB * (FB // 2) - 3 * (KB - m) + ch + 1)

        def pool_ln(p, q, mixed, s, hs):
            for m in range(1, KB - 1):
                mixed(p, m, NCH - 1)
                if m > 1:
                    need(p, sum_rdy, (KB - 2) * q + m - 1)
                else:
                    need(p, mean_ps, 3 * q)
                p.tensor_tensor(SUMX[:, :], X[:, 0, :] if m == 1 else SUMX[:, :], X[:, m, :], ALU.add).then_inc(sum_rdy, 1)
            if hs is not None:
                for ch in range(NCH):
                    p.wait_ge(x_rdy, 3 * q + ch + 1)
                    make_hin(p, s, hs, ch)

        def pe_ln(e, q, mixed):
            for ch, (c0, cw) in enumerate(CHS):
                mixed(e, KB - 1, ch)
                e.wait_ge(sum_rdy, (KB - 2) * (q + 1))
                e.matmul(PS[:, ch, 0:cw], con(C_ONE), SUMX[:, c0:c0 + cw], start=True, stop=False)
                e.matmul(PS[:, ch, 0:cw], con(C_ONE), X[:, KB - 1, c0:c0 + cw], start=False, stop=True).then_inc(mean_ps, 1)
            for ch, (c0, cw) in enumerate(CHS):
                e.wait_ge(lsq_rdy, 3 * q + ch + 1)
                for b in range(KB):
                    mm = e.matmul(PS[:, 3 + ch, 0:cw], con(C_ONE), SQL[ch % 2][:, b, 0:cw], start=(b == 0), stop=(b == KB - 1))
                mm.then_inc(var_ps, 1)

        def act_ln(a, q, hin):
            def square(ch):
                c0, cw = CHS[ch]
                a.wait_ge(cen_rdy, 3 * q + ch + 1)
                if ch == 2:
                    a.wait_ge(var_ps, 3 * q + 1)
                a.activation(SQL[ch % 2][:, :, 0:cw], X[:, :, c0:c0 + cw], ACT.Square).then_inc(lsq_rdy, 1)

            def root(ch):
                c0, cw = CHS[ch]
                a.wait_ge(var_ps, 3 * q + ch + 1)
                a.activation(RST[:, ch, 0:cw], PS[:, 3 + ch, 0:cw], ACT.Sqrt, scale=1.0 / D, bias=EPS[:, 0:1]).then_inc(std_rdy, 1)

            def affine(ch):
                c0, cw = CHS[ch]
                a.wait_ge(nrl_rdy, 3 * q + ch + 1)
                for b in range(KB):
                    ins = a.activation(X[:, b, c0:c0 + cw], (TB, TB1, TB2)[ch][:, b, 0:cw], ACT.Identity,
                                       scale=PAR[:, P_LNG + KB * q + b:P_LNG + KB * q + b + 1],
                                       bias=PAR[:, P_LNB + KB * q + b:P_LNB + KB * q + b + 1])
                ins.then_inc(x_rdy, 1)
            square(0)
            square(1)
            root(0)
            square(2)
            root(1)
            root(2)
            affine(0)
            affine(1)
            hin(0)
            affine(2)
            hin(1)
            hin(2)

        def vec_ln(v, q, mixed, hs):
            mixed(v, KB - 1, NCH - 1)
            for ch, (c0, cw) in enumerate(CHS):
                v.wait_ge(mean_ps, 3 * q + ch + 1)
                v.scalar_tensor_tensor(X[:, :, c0:c0 + cw], PS[:, ch, 0:cw].unsqueeze(1).to_broadcast([128, KB, cw]), -1.0 / D,
                                       X[:, :, c0:c0 + cw], ALU.mult, ALU.add).then_inc(cen_rdy, 1)
            for ch, (c0, cw) in enumerate(CHS):
                v.wait_ge(std_rdy, 3 * q + ch + 1)
                v.reciprocal(RST[:, ch, 0:cw], RST[:, ch, 0:cw]).then_inc(ln_g, 1)
                v.wait_ge(ln_g, 3 * q + ch + 1)
                v.wait_ge(cen_rdy, 3 * q + 3)
                v.tensor_tensor((TB, TB1, TB2)[ch][:, :, 0:cw], X[:, :, c0:c0 + cw], RST[:, ch, 0:cw].unsqueeze(1).to_broadcast([128, KB, cw]),
                                ALU.mult).then_inc(nrl_rdy, 1)
            if hs is not None:
                for ch in range(NCH):
                    vec_lower(v, hs, ch)

        NP = FB // 2

        def slab_of(n0, j, f, half):
            at = n0 + 6 * j - 2
            return at + (half if f == 0 else 4 + half)

        def up_index(j, f, half):
            return 4 * j + 2 * f + half

        def pe_ffn(e, l, n0, g0, hs):
            d0, x0 = l * 3 * KB * NP, l * FB

            def up(j, f, n, ready=None):
                for half in range(2):
                    u = (n0 + half) % 2
                    g = g0 + up_index(j, f, half)
                    dense(e, n + half, u, g, half, ready if half == 0 else None)

            def down(j, n):
                for m in range(KB):
                    if m % 4 == 0:
                        need(e, hi_done, n + m // 4 + 1)
                        need(e, lo_done, n + m // 4 + 1)
                    if m == 0:
                        need(e, fh_rdy, x0 + 2 * j + 2)
                        need(e, fl_rdy, x0 + 2 * j + 2)
                    u = (n0 + m // 4) % 2
                    for ch, (c0, cw) in enumerate(CHS):
                        k = 3 * m + ch
                        need(e, dn_ev, d0 + 3 * KB * j + k - 1)
                        for f in range(2):
                            mm = three(e, PS[:, 6 + k % 2, 0:cw], u, f * 512 + (m % 4) * 128, FH[:, f, c0:c0 + cw],
                                       FL[:, f, c0:c0 + cw], f == 0, f == 1, m % 4 == 0 and ch == 0 and f == 0)
                        mm.then_inc(dn_ps, 1)
            up(0, 0, n0, hin_ready(e, hs))
            up(0, 1, n0 + 2)
            with e.Fori(1, NP) as j:
                n = n0 + 4 + 6 * (j - 1)
                up(j, 0, n)
                down(j - 1, n + 2)
                up(j, 1, n + 4)
            down(NP - 1, n0 + 6 * NP - 2)

        def act_ffn(a, l, n0, g0):
            x0 = l * FB

            def copy_out(j, f, half):
                x = x0 + 2 * j + f
                g = g0 + up_index(j, f, half)
                if half == 0:
                    need(a, cf_rdy, x)
                    need(a, tlf_rdy, x)
                    need(a, psf_rdy, x + 1)
                bias = PSF[:, f, 7 * half:7 * half + 1]
                for ch, (c0, cw) in enumerate(CHS):
                    need(a, up_done, 3 * g + ch + 1)
                    src = PS[:, 3 * half + ch, :]
                    if c0 + cw <= SEQ:
                        a.activation(UF[:, half, GAP + c0:GAP + c0 + cw], src[:, 0:cw], ACT.Identity, bias=bias).then_inc(up_ev, 1)
                    else:
                        a.activation(UF[:, half, GAP + c0:GAP + SEQ], src[:, 0:SEQ - c0], ACT.Identity, bias=bias)
                        a.activation(UF[:, half, GAP + SAM:GAP + T], src[:, SAM - c0:T - c0], ACT.Identity, bias=bias).then_inc(up_ev, 1)

            def silu(j, f):
                need(a, cf_rdy, x0 + 2 * j + f + 1)
                a.activation(CF[:, 0, :], CF[:, 0, :], ACT.Silu, bias=PSF[:, f, 4:5]).then_inc(sil_rdy, 1)

            def upper(j, f):
                need(a, ft_rdy, x0 + 2 * j + f + 1)
                need(a, dn_ps, l * 3 * KB * NP + 3 * KB * j)
                a.activation(FH[:, f, :], FT[:, :], ACT.Copy).then_inc(fh_rdy, 1)

            def split(n, k):
                split_hi(a, n + k, (n0 + k) % 2)
            split(n0, 1)
            copy_out(0, 0, 0)
            split(n0, 2)
            copy_out(0, 0, 1)
            split(n0, 3)
            silu(0, 0)
            upper(0, 0)
            copy_out(0, 1, 0)
            split(n0, 4)
            copy_out(0, 1, 1)
            split(n0, 5)
            silu(0, 1)
            upper(0, 1)

            def pair(j, last):
                n = n0 + 4 + 6 * (j - 1)
                copy_out(j, 0, 0)
                split(n, 2)
                copy_out(j, 0, 1)
                split(n, 3)
                split(n, 4)
                silu(j, 0)
                upper(j, 0)
                split(n, 5)
                copy_out(j, 1, 0)
                split(n, 6)
                copy_out(j, 1, 1)
                if not last:
                    split(n, 7)
                silu(j, 1)
                upper(j, 1)
                if last:
                    split(n, 7)
            with a.Fori(1, NP - 1) as j:
                pair(j, False)
            pair(NP - 1, True)

        def pool_ffn(p, l, n0, g0, hs):
            x0 = l * FB

            def params(j, f):
                x = x0 + 2 * j + f
                need(p, cf_rdy, x)
                need(p, ft_rdy, x)
                p.tensor_copy(PSF[:, f, :], PAR[:, ds(P_FFN + FPW * (l * FB + 2 * j + f), FPW)])
                ins = p.tensor_copy(UF[:, :, GAP + SAM - (FC - 1):GAP + SAM],
                                    PAR[:, ds(P_FFN + FPW * (l * FB + 2 * j + f), FPW)].rearrange("p (x c) -> p x c", x=2)[:, :, 5:7])
                ins.then_inc(psf_rdy, 1)

            def tails(j, f):
                need(p, up_ev, 3 * (g0 + up_index(j, f, 1)) + 3)
                w = GAP + DEC
                for half in range(2):
                    src = UF[:, half, SEQ + GAP - w:GAP + T].rearrange("p (s c) -> p s c", s=2)[:, :, w - (FC - 1):]
                    ins = p.tensor_copy(TLF[:, ds(2 * j + f, 1), half, :, :].rearrange("p a s c -> p (a s) c"), src)
                ins.then_inc(tlf_rdy, 1)

            def split(n, k):
                split_lo(p, n + k, (n0 + k) % 2)
            need(p, hl_rdy, 3 * hs + 3)
            p.memset(UF[:, :, 0:GAP], 0.0)
            p.memset(UF[:, :, GAP + SEQ:GAP + SAM - (FC - 1)], 0.0)
            params(0, 0)
            split(n0, 1)
            split(n0, 2)
            tails(0, 0)
            split(n0, 3)
            params(0, 1)
            split(n0, 4)
            tails(0, 1)
            split(n0, 5)
            with p.Fori(1, NP) as j:
                n = n0 + 4 + 6 * (j - 1)
                params(j, 0)
                split(n, 2)
                tails(j, 0)
                split(n, 3)
                split(n, 4)
                params(j, 1)
                split(n, 5)
                split(n, 6)
                tails(j, 1)
                split(n, 7)

        def vec_ffn(v, l, s, g0):
            x0, d0 = l * FB, l * 3 * KB * NP

            def conv(j, f):
                x = x0 + 2 * j + f
                need(v, psf_rdy, x + 1)
                need(v, up_ev, 3 * (g0 + up_index(j, f, 1)) + 3)
                need(v, ft_rdy, x)
                for t in range(FC):
                    for half in range(2):
                        src = UF[:, half, GAP - (FC - 1) + t:GAP - (FC - 1) + t + T]
                        w = PSF[:, f, 7 * half + 1 + t:7 * half + 2 + t]
                        if t == 0:
                            ins = v.tensor_scalar(CF[:, half, :], src, w, None, ALU.mult)
                        else:
                            v.wait_ge(cf_ch, 5 * x + 2 * (t - 1) + half + 1)
                            ins = v.scalar_tensor_tensor(CF[:, half, :], src, w, CF[:, half, :], ALU.mult, ALU.add)
                        ins.then_inc(cf_rdy if (t, half) == (2, 1) else cf_ch, 1)
                        yield

            def gate(j, f):
                x = x0 + 2 * j + f
                need(v, sil_rdy, x + 1)
                need(v, cf_rdy, x + 1)
                need(v, fl_rdy, x)
                need(v, fh_rdy, x)
                v.scalar_tensor_tensor(FT[:, :], CF[:, 1, :], PSF[:, f, 11:12], CF[:, 0, :], ALU.add, ALU.mult).then_inc(ft_rdy, 1)

            def lower(j, f):
                x = x0 + 2 * j + f
                need(v, fh_rdy, x + 1)
                need(v, ft_rdy, x + 1)
                v.tensor_tensor(FL[:, f, :], FT[:, :], FH[:, f, :].bitcast(fp32), ALU.subtract).then_inc(fl_rdy, 1)

            def mix(j, steps=iter(())):
                for m in range(KB):
                    for ch, (c0, cw) in enumerate(CHS):
                        k = 3 * m + ch
                        need(v, dn_ps, d0 + 3 * KB * j + k + 1)
                        for a, w, st in pieces(c0, cw):
                            ins = v.scalar_tensor_tensor(X[:, m, a:a + w], PS[:, 6 + k % 2, a - c0:a - c0 + w],
                                                         ADA[:, s, 2 * KB + m, st:st + 1], X[:, m, a:a + w], ALU.mult, ALU.add)
                        ins.then_inc(dn_ev, 1)
                        if k % 4 == 1:
                            next(steps, None)
                for _ in steps:
                    pass

            def every_step(steps):
                for _ in steps:
                    pass

            def one(j, f):
                every_step(conv(j, f))
                gate(j, f)
                lower(j, f)
            one(0, 0)
            one(0, 1)
            with v.Fori(1, NP) as j:
                mix(j - 1, conv(j, 0))
                gate(j, 0)
                lower(j, 0)
                one(j, 1)
            mix(NP - 1)

        def no_hin(ch):
            pass

        G_F0 = G_WO + KB
        G_M = G_F0 + 2 * FB

        G_Q, G_P = G_M + LB + 1, G_M + LB + 1 + QB
        G_MO = G_P + HEADS // 2
        G_F1 = G_MO + KB

        def all_here(e, *pairs):
            for s_, n_ in pairs:
                need(e, s_, n_)

        def act_rms(a, r, buf, nb, g):
            need(a, up_ev, 3 * g)

            def square(ch):
                c0, cw = CHS[ch]
                if ch == 2:
                    a.wait_ge(msum_ps, 3 * r + 1)
                a.activation(SQM[:, ch % 2, 0:nb, 0:cw], buf[:, :, c0:c0 + cw], ACT.Square).then_inc(msq_rdy, 1)

            def root(ch):
                c0, cw = CHS[ch]
                a.wait_ge(msum_ps, 3 * r + ch + 1)
                if ch == 2:
                    a.wait_ge(mnrm_rdy, 3 * r + 1)
                a.activation(RSM[:, ch % 2, 0:cw], PS[:, 6 + ch % 2, 0:cw], ACT.Sqrt, scale=1.0 / (128 * nb), bias=EPS[:, 1:2]).then_inc(mstd_rdy, 1)
            square(0)
            square(1)
            root(0)
            square(2)
            root(1)
            root(2)

        def pe_rms(e, r, nb):
            for ch, (c0, cw) in enumerate(CHS):
                e.wait_ge(msq_rdy, 3 * r + ch + 1)
                e.wait_ge(rot_ev, 3 * r)
                if ch == 2:
                    e.wait_ge(mstd_rdy, 3 * r + 1)
                for b in range(nb):
                    mm = e.matmul(PS[:, 6 + ch % 2, 0:cw], con(C_ONE), SQM[:, ch % 2, b, 0:cw], start=(b == 0), stop=(b == nb - 1))
                mm.then_inc(msum_ps, 1)

        def vec_rms(v, r, buf, nb, gain):
            for ch, (c0, cw) in enumerate(CHS):
                v.wait_ge(mstd_rdy, 3 * r + ch + 1)
                v.reciprocal(RSM[:, ch % 2, 0:cw], RSM[:, ch % 2, 0:cw]).then_inc(mrc_rdy, 1)
                v.wait_ge(mrc_rdy, 3 * r + ch + 1)
                for b in range(nb):
                    ins = v.scalar_tensor_tensor(buf[:, b, c0:c0 + cw], buf[:, b, c0:c0 + cw], PAR[:, gain + b:gain + b + 1],
                                                 RSM[:, ch % 2, 0:cw], ALU.mult, ALU.mult)
                ins.then_inc(mnrm_rdy, 1)

        def pe_rope(e, z, buf, g):
            for ch, (c0, cw) in enumerate(CHS):
                need(e, up_ev, 3 * g + ch + 1)
                e.wait_ge(mstd_rdy, 3 if z == 0 else 6)
                if 3 * z + ch >= 2:
                    e.wait_ge(rot_ev, 3 * z + ch - 1)
                e.matmul(PS[:, 6 + (3 * z + ch) % 2, 0:cw], con(C_ROT), buf[:, c0:c0 + cw], start=True, stop=True).then_inc(rot_ps, 1)

        def vec_rope(v, z, buf, tmp):
            for ch, (c0, cw) in enumerate(CHS):
                n = 3 * z + ch + 1
                v.wait_ge(rot_ps, n)
                if z == 0:
                    v.wait_ge(kv_ld, 48)
                v.tensor_tensor(tmp[:, c0:c0 + cw], PS[:, 6 + (3 * z + ch) % 2, 0:cw], COSN[:, 1, c0:c0 + cw], ALU.mult).then_inc(rot_ev, 1)
                v.tensor_tensor(buf[:, c0:c0 + cw], buf[:, c0:c0 + cw], COSN[:, 0, c0:c0 + cw], ALU.mult).then_inc(rot_ch, 1)
                v.wait_ge(rot_ev, n)
                v.wait_ge(rot_ch, n)
                v.tensor_tensor(buf[:, c0:c0 + cw], buf[:, c0:c0 + cw], tmp[:, c0:c0 + cw], ALU.add).then_inc(rope_rdy, 1)

        def act_evac(a, g, out):
            for ch, (c0, cw) in enumerate(CHS):
                need(a, up_done, 3 * g + ch + 1)
                a.activation(out[:, c0:c0 + cw], PS[:, 3 * (g % 2) + ch, 0:cw], ACT.Copy).then_inc(up_ev, 1)

        QTILES = [(128 * t, 128, 0, 128 * (t + 1)) for t in range(GT)] + [(SAM, DEC, SAM, SKEYS)]
        NQ = GT + 1
        BIG = [t for t in range(NQ) if QTILES[t][3] > 512]

        def nbig(t):
            return len([x for x in BIG if x < t])

        def key_blocks(t):
            q0, P, k0, nk = QTILES[t]
            first = 0 if t < GT else GT
            return [(first + m, min(128, nk - 128 * m)) for m in range(-(-nk // 128))]

        def scores(t):
            q0, P, k0, nk = QTILES[t]
            return PS[0:P, 2 * (t % 2):2 * (t % 2) + 2, :].rearrange("p b c -> p (b c)")[:, 0:nk]

        V_TILES = [128 * t for t in range(GT)] + [SAM + 128 * m for m in range((KPAD - SAM) // 128)]
        V_BANK = (7, 0, 1)

        def pe_head(e, i, u):
            h = 2 * i + u
            n, w = S_HD + h, (S_HD + u) % 2
            all_here(e, (hi_done, n + 1), (lo_done, n + 1))
            if u == 0:
                all_here(e, (qc_rdy, i + 1))
            all_here(e, (ex_rdy, NQ * h), (pt_ev, NQ * h), (pu_ev, len(BIG) * h), (ov_ev, NQ * h))
            for ch, (c0, cw) in enumerate(CHS):
                for k in range(QB):
                    mm = three(e, PS[:, ch, 0:cw], w, k * 128, QLH[:, k, c0:c0 + cw], QLL[:, k, c0:c0 + cw], k == 0, k == QB - 1,
                               ch == 0 and k == 0)
                mm.then_inc(pj_ps, 1)
            for ch, (c0, cw) in enumerate(KCH):
                for k in range(LB):
                    mm = three(e, PS[:, 3 + ch, 0:cw], w, 128 * (QB + k), CKH[:, k, c0:c0 + cw], CKL[:, k, c0:c0 + cw], k == 0, k == LB - 1)
                mm.then_inc(pj_ps, 1)
            for t, c0 in enumerate(V_TILES):
                if t % 4 == 0 and t:
                    all_here(e, (qv_ev, 6 * h + t // 4))
                out = PS[:, V_BANK[t // 4], (t % 4) * 128:(t % 4) * 128 + 128]
                for k in range(LB):
                    c = 128 * (QB + LB + k)
                    e.matmul(out, CKH[:, k, c0:c0 + 128], WH[w][:, c:c + 128], start=(k == 0), stop=False)
                    e.matmul(out, CKH[:, k, c0:c0 + 128], WL[w][:, c:c + 128], start=False, stop=False)
                    mm = e.matmul(out, CKL[:, k, c0:c0 + 128], WH[w][:, c:c + 128], start=False, stop=(k == LB - 1))
                if t % 4 == 3 or t == len(V_TILES) - 1:
                    mm.then_inc(pj_ps, 1)
            all_here(e, (qv_ev, 6 * h + 6), (k_ev, 4 * h + 4))

            def score(t):
                q0, P, k0, nk = QTILES[t]
                if t >= 2:
                    all_here(e, (ex_rdy, NQ * h + t - 1))
                for s0_ in range(0, nk, 512):
                    w_ = min(512, nk - s0_)
                    out = PS[0:P, 2 * (t % 2) + s0_ // 512, :]
                    last = s0_ + w_ == nk and t < GT
                    e.matmul(out[:, 0:w_], QT[:, q0:q0 + P], KT[:, k0 + s0_:k0 + s0_ + w_], start=True, stop=False)
                    mm = e.matmul(out[:, 0:w_], QPC[64 * u:64 * u + 64, q0:q0 + P], KPE[64 * u:64 * u + 64, k0 + s0_:k0 + s0_ + w_],
                                  start=False, stop=not last)
                    if last:
                        mm = e.matmul(out[:, w_ - 128:w_], MSK[0:1, 0, :], MSK[0:1, 1, :], start=False, stop=True)
                mm.then_inc(sc_ps, 1)
            score(0)
            score(1)
            for t in range(NQ):
                q0, P, k0, nk = QTILES[t]
                blocks = key_blocks(t)
                all_here(e, (nm_rdy, NQ * h + t + 1), (pt_ev, NQ * h + t), (pu_ev, len(BIG) * h + nbig(t)))
                if P < 128:
                    e.sem_inc(pe_step, 1)
                for m, (b, kw) in enumerate(blocks):
                    mm = e.transpose(PS[0:kw, 4 + m // 4, (m % 4) * 128:(m % 4) * 128 + P], PR[t % 2][0:P, 128 * m:128 * m + kw], con(C_ID, P, P))
                    if m == min(4, len(blocks)) - 1:
                        mm.then_inc(pt_ps, 1)
                if t in BIG:
                    mm.then_inc(pu_ps, 1)
                if t + 2 < NQ:
                    score(t + 2)
                all_here(e, (pt_ev, NQ * h + t + 1), (pu_ev, len(BIG) * h + nbig(t + 1)))
                if t >= 2:
                    all_here(e, (ov_ev, NQ * h + t - 1))
                for m, (b, kw) in enumerate(blocks):
                    mm = e.matmul(PS[:, 6 + t % 2, 0:P], VT[0:kw, b, :], PT[0:kw, m, 0:P], start=(m == 0), stop=(m == len(blocks) - 1))
                mm.then_inc(ov_ps, 1)

        def act_head(a, i, u):
            h = 2 * i + u
            split_hi(a, S_HD + h + 1, (S_HD + u + 1) % 2)
            for ch, (c0, cw) in enumerate(CHS):
                all_here(a, (pj_ps, 10 * h + ch + 1))
                a.activation(QT[:, c0:c0 + cw], PS[:, ch, 0:cw], ACT.Copy).then_inc(qv_ev, 1)
            for m, b in enumerate(V_BANK):
                all_here(a, (pj_ps, 10 * h + 8 + m))
                nt = min(4, len(V_TILES) - 4 * m)
                a.activation(VT[:, 4 * m:4 * m + nt, :], PS[:, b, 0:128 * nt].rearrange("p (t c) -> p t c", c=128), ACT.Copy).then_inc(qv_ev, 1)

            def weights(t):
                q0, P, k0, nk = QTILES[t]
                all_here(a, (mx_rdy, 2 * (NQ * h + t) + 2))
                if t >= 2:
                    all_here(a, (pt_ps, NQ * h + t - 1), (pu_ps, len(BIG) * h + nbig(t - 1)))
                a.activation(PR[t % 2][0:P, 0:nk], scores(t), ACT.Exp, scale=SCALE, bias=SMX[0:P, 1, t:t + 1],
                             accum_out=SMX[0:P, 2, t:t + 1]).then_inc(ex_rdy, 1)
            weights(0)
            weights(1)
            for t in range(NQ):
                q0, P, k0, nk = QTILES[t]
                all_here(a, (pt_ps, NQ * h + t + 1))
                if t:
                    all_here(a, (ov_ps, NQ * h + t))
                full = [m for m, (b, kw) in enumerate(key_blocks(t)) if kw == 128 and m < 4]
                rest = [(m, kw) for m, (b, kw) in enumerate(key_blocks(t)) if kw < 128]
                ins = a.activation(PT[:, 0:len(full), 0:P], bank(4, 128, P)[:, 0:len(full), :], ACT.Copy)
                for m, kw in rest:
                    ins = a.activation(PT[0:kw, m, 0:P], PS[0:kw, 4, m * 128:m * 128 + P], ACT.Copy)
                ins.then_inc(pt_ev, 1)
                if t + 2 < NQ:
                    weights(t + 2)
                all_here(a, (ov_ps, NQ * h + t + 1))
                if t == 0:
                    all_here(a, (o_st[u], 16 * i))
                a.activation(OH[u][:, q0:q0 + P], PS[:, 6 + t % 2, 0:P], ACT.Copy).then_inc(ov_ev, 1)
            all_here(a, (ov_ev, NQ * h + NQ))
            a.dma_start(scr[ds(h, 1), :, :].rearrange("a p n -> p (a n)"), OH[u][:, :]).then_inc(o_st[u], 16)

        def vec_head(v, i, u):
            h = 2 * i + u
            for ch, (c0, cw) in enumerate(KCH):
                all_here(v, (pj_ps, 10 * h + 4 + ch))
                v.tensor_copy(KT[:, c0:c0 + cw], PS[:, 3 + ch, 0:cw]).then_inc(k_ev, 1)

            def top(t):
                q0, P, k0, nk = QTILES[t]
                x = NQ * h + t
                all_here(v, (sc_ps, x + 1))
                v.tensor_reduce(SMX[0:P, 0, t:t + 1], scores(t), AX.X, ALU.max).then_inc(mx_rdy, 1)
                all_here(v, (mx_rdy, 2 * x + 1))
                v.tensor_scalar(SMX[0:P, 1, t:t + 1], SMX[0:P, 0, t:t + 1], -SCALE, None, ALU.mult).then_inc(mx_rdy, 1)

            def normalise(t):
                q0, P, k0, nk = QTILES[t]
                x = NQ * h + t
                all_here(v, (ex_rdy, x + 1))
                v.reciprocal(SMX[0:P, 3, t:t + 1], SMX[0:P, 2, t:t + 1]).then_inc(mrc_rdy, 1)
                all_here(v, (mrc_rdy, 6 + x + 1))
                v.tensor_scalar(PR[t % 2][0:P, 0:nk], PR[t % 2][0:P, 0:nk], SMX[0:P, 3, t:t + 1], None, ALU.mult).then_inc(nm_rdy, 1)
            top(0)
            top(1)
            normalise(0)
            for t in range(NQ):
                if t + 1 < NQ:
                    normalise(t + 1)
                if t in BIG:
                    all_here(v, (pu_ps, len(BIG) * h + nbig(t) + 1), (ov_ps, NQ * h + t))
                    nb = len(key_blocks(t)) - 4
                    v.tensor_copy(PT[:, 4:4 + nb, :], bank(5)[:, 0:nb, :]).then_inc(pu_ev, 1)
                if t + 2 < NQ:
                    top(t + 2)

        def pool_head(p, i, u):
            h = 2 * i + u
            if u == 0:
                all_here(p, (sc_ps, NQ * h))
                p.tensor_copy(QPC[:, :], QPE[:, ds(i, 1), :].rearrange("p a c -> p (a c)")).then_inc(qc_rdy, 1)
            split_lo(p, S_HD + h + 1, (S_HD + u + 1) % 2)

        def pe_rest(e):
            pe_gate(e)
            pe_proj(e, S_WO, G_WO, all_of(e, (oh_rdy, 8), (ol_rdy, 8), (rb_ev, 24)))
            pe_ln(e, 0, mixed_up(G_WO))
            pe_ffn(e, 0, S_F0, G_F0, 1)
            pe_ln(e, 1, mixed_down(0))
            for b in range(LB + 1):
                dense(e, S_KV + b, (S_KV + b) % 2, G_M + b, (G_M + b) % 2, hin_ready(e, 2) if b == 0 else None)
            pe_rms(e, 0, LB)
            pe_rope(e, 0, KPE, G_M + LB)
            for b in range(QB):
                dense(e, S_DQ + b, (S_DQ + b) % 2, G_Q + b, (G_Q + b) % 2, hin_ready(e, 3) if b == 0 else None)
            pe_rms(e, 1, QB)
            for b in range(HEADS // 2):
                n = S_QP + b // 2
                dense(e, n, n % 2, G_P + b, (G_P + b) % 2, all_of(e, (lh_rdy, 2), (ll_rdy, 2)) if b == 0 else None,
                      QB, QLH, QLL, (b % 2) * QB * 128, b % 2 == 0)
            for b in range(HEADS // 2):
                pe_rope(e, b + 1, QPE[:, b, :], G_P + b)
            all_here(e, (rot_ev, 15), (c_ld, 48), (rope_rdy, 15))
            with e.Fori(0, HEADS // 2) as i:
                for u in range(2):
                    pe_head(e, i, u)
            all_here(e, (ov_ev, NQ * HEADS))
            pe_proj(e, S_MO, G_MO, hin_ready(e, 4))
            pe_ln(e, 2, mixed_up(G_MO))
            pe_ffn(e, 1, S_F1, G_F1, 5)
            pe_ln(e, 3, mixed_down(1))

        def act_rest(a):
            act_gate(a)
            act_split_run(a, S_WO + 1, KB)
            act_ln(a, 0, act_hin_chunk(a, 1))
            act_ffn(a, 0, S_F0, G_F0)
            split_hi(a, S_KV, S_KV % 2)
            a.wait_ge(tlf_rdy, FB)
            a.dma_start(o_fcv[0], TLF[:, :, :, :, :]).then_inc(out_done, 16)
            a.wait_ge(out_done, 64)
            act_ln(a, 1, act_hin_chunk(a, 2))
            a.wait_ge(hl_rdy, 9)
            a.dma_start(CKF[:, :, T:KEYS], pckv).then_inc(kv_ld, 16)
            a.dma_start(KPE[:, T:KEYS], pkpe).then_inc(kv_ld, 16)
            a.dma_start(COSN[:, :, :], cs).then_inc(kv_ld, 16)
            for b in range(LB + 1):
                split_hi(a, S_KV + b + 1, (S_KV + b + 1) % 2)
                act_evac(a, G_M + b, CKF[:, b, :] if b < LB else KPE)
            act_rms(a, 0, CKF, LB, G_M + LB + 1)
            a.wait_ge(mnrm_rdy, 3)
            a.dma_start(o_ckv, CKF[:, :, 0:T]).then_inc(out_done, 16)
            every(act_hin_chunk(a, 3))
            all_here(a, (out_done, 80), (kv_ld, 48), (pad_rdy, 1))
            a.activation(CKH[:, :, :], CKF[:, :, :], ACT.Copy).then_inc(lh_rdy, 1)
            a.wait_ge(rope_rdy, 3)
            a.dma_start(o_kpe, KPE[0:ROPE, 0:T]).then_inc(out_done, 16)
            for b in range(QB):
                split_hi(a, S_DQ + b + 1, (S_DQ + b + 1) % 2)
                act_evac(a, G_Q + b, QLF[:, b, :])
            act_rms(a, 1, QLF, QB, G_Q + QB)
            a.wait_ge(mnrm_rdy, 6)
            a.activation(QLH[:, :, :], QLF[:, :, :], ACT.Copy).then_inc(lh_rdy, 1)
            for b in range(HEADS // 2):
                if b % 2 == 0:
                    split_hi(a, S_QP + b // 2 + 1, (S_QP + b // 2 + 1) % 2)
                act_evac(a, G_P + b, QPE[:, b, :])
            a.dma_start(MSK[:, :, :], msk).then_inc(c_ld, 16)
            with a.Fori(0, HEADS // 2) as i:
                for u in range(2):
                    act_head(a, i, u)
            for u in range(2):
                all_here(a, (o_st[u], 16 * HEADS // 2))
            for ch, (c0, cw) in enumerate(CHS):
                a.dma_start(OL[ch][:, :, 0:cw], scr[0:HEADS, :, c0:c0 + cw].rearrange("h p t -> p h t")).then_inc(o_ld[ch], 16)
            for ch, (c0, cw) in enumerate(CHS):
                a.wait_ge(o_ld[ch], 16)
                a.activation(HH[:, :, c0:c0 + cw], OL[ch][:, :, 0:cw], ACT.Copy).then_inc(hh_rdy, 1)
            act_split_run(a, S_MO + 1, KB)
            act_ln(a, 2, act_hin_chunk(a, 5))
            a.wait_ge(out_done, 96)
            act_ffn(a, 1, S_F1, G_F1)
            a.wait_ge(tlf_rdy, 2 * FB)
            a.dma_start(o_fcv[1], TLF[:, :, :, :, :]).then_inc(out_done, 16)
            a.wait_ge(out_done, 112)
            act_ln(a, 3, no_hin)

        def pool_rest(p):
            pool_gate(p)
            pool_split_run(p, S_WO + 1, KB)
            pool_ln(p, 0, mixed_up(G_WO), 1, 1)
            pool_ffn(p, 0, S_F0, G_F0, 1)
            pool_split_run(p, S_KV, 1)
            pool_ln(p, 1, mixed_down(0), None, 2)
            p.wait_ge(hl_rdy, 9)
            p.memset(CKF[:, :, KEYS:], 0.0).then_inc(pad_rdy, 1)
            pool_split_run(p, S_KV + 1, S_HD - S_KV)
            all_here(p, (up_ev, 3 * G_MO), (rope_rdy, 15))
            for u in range(2):
                ins = p.memset(OH[u][:, SEQ:SAM], 0.0)
            with p.Fori(0, HEADS // 2) as i:
                for u in range(2):
                    pool_head(p, i, u)
            pool_split_run(p, S_MO + 1, KB)
            pool_ln(p, 2, mixed_up(G_MO), 3, 5)
            pool_ffn(p, 1, S_F1, G_F1, 5)
            pool_ln(p, 3, mixed_down(1), None, None)

        def vec_rest(v):
            vec_gate(v)
            vec_proj(v, 0, G_WO)
            vec_ln(v, 0, mixed_up(G_WO), 1)
            vec_ffn(v, 0, 1, G_F0)
            vec_ln(v, 1, mixed_down(0), 2)
            vec_rms(v, 0, CKF, LB, P_KVG)
            vec_rope(v, 0, KPE, QLF[:, 0, :])
            every(vec_hin_chunk(v, 2, 3))
            v.wait_ge(lh_rdy, 1)
            v.tensor_tensor(CKL[:, :, :], CKF[:, :, :], CKH[:, :, :].bitcast(fp32), ALU.subtract).then_inc(ll_rdy, 1)
            vec_rms(v, 1, QLF, QB, P_QG)
            v.wait_ge(lh_rdy, 2)
            v.tensor_tensor(QLL[:, :, :], QLF[:, :, :], QLH[:, :, :].bitcast(fp32), ALU.subtract).then_inc(ll_rdy, 1)
            for b in range(HEADS // 2):
                vec_rope(v, b + 1, QPE[:, b, :], QT)
            with v.Fori(0, HEADS // 2) as i:
                for u in range(2):
                    vec_head(v, i, u)
            for ch, (c0, cw) in enumerate(CHS):
                v.wait_ge(hh_rdy, 12 + ch + 1)
                v.tensor_tensor(HL[:, :, c0:c0 + cw], OL[ch][:, :, 0:cw], HH[:, :, c0:c0 + cw].bitcast(fp32), ALU.subtract).then_inc(hl_rdy, 1)
            vec_proj(v, 2, G_MO)
            vec_ln(v, 2, mixed_up(G_MO), 5)
            vec_ffn(v, 1, 3, G_F1)
            vec_ln(v, 3, mixed_down(1), None)

        def final_outputs(sp):
            for ch, (c0, cw) in enumerate(CHS):
                sp.wait_ge(x_rdy, 9 + ch + 1)
                sp.dma_start(y[:, :, c0:c0 + cw], X[:, :, c0:c0 + cw]).then_inc(y_st, 16)
            sp.wait_ge(y_st, 16 * NCH)
            sp.wait_ge(out_done, 112)

        block = ctx.enter_context(nc.Block())

        @block.sync
        def _(sp):
            sp.dma_start(CT[:, :, :], cT).then_inc(c_ld, 16)
            for t in range(3):
                sp.dma_start(AD0[t][:, :, :], wada0[:, KB * t:KB * t + KB, :]).then_inc(ada0_ld[t], 16)
            sp.dma_start(PAR[:, :], par).then_inc(par_ld, 16)
            sp.dma_start(X[:, :, :], xT).then_inc(x_ld, 16)
            sp.dma_start(CST[:, :, :], cst).then_inc(par_ld, 16)

            def load(n, u, wait=True):
                if wait:
                    need(sp, hi_done, n - 1)
                    need(sp, lo_done, n - 1)
                sp.dma_start(RAW[:, u, :], ws[ds(n, 1), :, :].rearrange("a p n -> p (a n)")).then_inc(raw_ld[u], 16)
            load(0, 0, False)
            load(1, 1, False)
            for s_, k in CREDIT.items():
                sp.sem_inc(s_, k)
            with sp.Fori(1, NSLAB // 2) as i:
                for u in range(2):
                    load(2 * i + u, u)
            if NSLAB % 2:
                load(NSLAB - 1, 0)
            final_outputs(sp)

        @block.scalar
        def _(act):
            act.wait_ge(c_ld, 16)
            act.activation(SC[:, :, :], CT[:, :, :], ACT.Silu).then_inc(sc_done, 1)
            split_hi(act, 0, 0)
            every(act_hin_chunk(act, 0))
            need(act, hl_rdy, 3)
            act.dma_start(CB[:, :, :], cB).then_inc(cb_ld, 16)
            act.wait_ge(cb_ld, 16)
            act.activation(CB[:, :, :], CB[:, :, :], ACT.Silu).then_inc(cb_rdy, 1)
            split_hi(act, 1, 1)

            def body(i, z):
                for u in range(2):
                    n = 2 * i + u
                    load_ada(act, n, u, z)
                    for ch, (c0, cw) in enumerate(CHS):
                        need(act, up_done, 3 * n + ch + 1)
                        if z:
                            if ch == 0:
                                need(act, v_st[u], 16 * i)
                            act.activation(VV[u][:, c0:c0 + cw], PS[:, 3 * u + ch, 0:cw], ACT.Silu).then_inc(up_ev, 1)
                            continue
                        if ch == 0:
                            need(act, conv_done, n - 1)
                            need(act, tail_rdy, n - 1)
                        if c0 + cw <= SEQ:
                            act.activation(UB[u][:, GAP + c0:GAP + c0 + cw], PS[:, 3 * u + ch, 0:cw], ACT.Copy).then_inc(up_ev, 1)
                        else:
                            act.activation(UB[u][:, GAP + c0:GAP + SEQ], PS[:, 3 * u + ch, 0:SEQ - c0], ACT.Copy)
                            act.activation(UB[u][:, GAP + SAM:GAP + T], PS[:, 3 * u + ch, SAM - c0:T - c0], ACT.Copy).then_inc(up_ev, 1)
                    split_hi(act, n + 2, u)
                    if z:
                        need(act, up_ev, 3 * n + 3)
                    else:
                        need(act, conv_done, n + 1)
                        need(act, v_st[u], 16 * i)
                        act.activation(VV[u][:, :], CV[u][:, :], ACT.Silu).then_inc(v_done, 1)
                        need(act, v_done, n + 1)
                    act.dma_start(scr[ds(n, 1), :, :].rearrange("a p n -> p (a n)"), VV[u][:, :]).then_inc(v_st[u], 16)
            with act.Fori(0, QKVB // 2) as i:
                body(i, False)
            with act.Fori(QKVB // 2, (QKVB + ZB) // 2) as i:
                body(i, True)
            n = QKVB + ZB
            for ch, (c0, cw) in enumerate(CHS):
                need(act, up_done, 3 * n + ch + 1)
                act.activation(AB[:, c0:c0 + cw], PS[:, ch, 0:cw], ACT.Copy).then_inc(up_ev, 1)
            need(act, ab_ps, 1)
            act.activation(BETAG[:, :, 8:16], PS[:, 0, 0:(GT + 1) * 16].rearrange("p (t c) -> p t c", c=16)[:, :, 0:8], ACT.Sigmoid).then_inc(gx, 1)
            need(act, bg_rdy, 4)
            act.activation(GX[:, 2], GX[:, 1], ACT.Exp).then_inc(gx, 1)
            need(act, gx, 2)
            act.activation(GX[:, 2], GX[:, 2], ACT.Ln, bias=1.0).then_inc(gx, 1)
            act.activation(AL[:, :], PAR[:, P_ALOG:P_ALOG + 8], ACT.Exp).then_inc(gx, 1)
            for u in range(2):
                need(act, v_st[u], 16 * (QKVB + ZB) // 2)
            need(act, tail_rdy, QKVB)
            act.dma_start(o_gcv, TAIL[:, :, :, :]).then_inc(out_done, 16)
            act.wait_ge(out_done, 16)
            act.dma_start(SS0[:, :, :], s0).then_inc(s0_ld, 16)
            load_qkv(act, 0, 128)
            with act.Fori(0, GT - 1) as i:
                act_g(act, i, PROMPT_TILE, 128)
            act_g(act, GT - 1, PROMPT_TILE, DEC)
            act_g(act, GT, SAMPLE_TILE, None)
            need(act, s_rdy, 4 * GT + 2)
            act.dma_start(o_gdn, SP0[:, :, :]).then_inc(out_done, 16)
            act.dma_start(s_gdn, SS0[:, :, :]).then_inc(out_done, 16)
            act_rest(act)

        @block.gpsimd
        def _(pool):
            for u in range(2):
                pool.memset(UB[u][:, 0:GAP], 0.0)
                pool.memset(UB[u][:, GAP + SEQ:GAP + SAM - (GC - 1)], 0.0)
            pool.memset(AB[:, T:], 0.0)
            pool.memset(EPS[:, 0:1], LN_EPS)
            pool.memset(EPS[:, 1:2], RMS_EPS).then_inc(ini, 1)
            split_lo(pool, 0, 0)
            split_lo(pool, 1, 1)
            pool.wait_ge(par_ld, 32)
            with pool.Fori(0, QKVB // 2) as i:
                for u in range(2):
                    n = 2 * i + u
                    need(pool, conv_done, n - 1)
                    c = PAR[:, ds(P_GCV + GPW * n, GPW)]
                    pool.tensor_copy(PST[:, u, :], c)
                    pool.tensor_copy(UB[u][:, GAP + SAM - (GC - 1):GAP + SAM], PAR[:, ds(P_GCV + GPW * n + GC, GC - 1)]).then_inc(pst_rdy, 1)
                    need(pool, up_ev, 3 * n + 3)
                    pool.tensor_copy(TAIL[:, ds(n, 1), :, :].rearrange("p a s c -> p (a s) c"), hist_cols(u)).then_inc(tail_rdy, 1)
                    split_lo(pool, n + 2, u)
            with pool.Fori(QKVB // 2, (QKVB + ZB) // 2) as i:
                for u in range(2):
                    split_lo(pool, 2 * i + u + 2, u)
            for u in range(2):
                need(pool, v_st[u], 16 * (QKVB + ZB) // 2)
            pool.memset(EXPO[:, :], -0.5)
            need(pool, ab_ps, 1)
            pool.memset(OUTT[:, :, SEQ:SAM], 0.0)
            pool.memset(SP0[:, :, :], 0.0).then_inc(g_ini, 1)
            pool.wait_ge(g_ini, 1)
            with pool.Fori(0, GT) as i:
                pool_g(pool, i, PROMPT_TILE, SP0)
            need(pool, s0_ld, 16)
            pool_g(pool, GT, SAMPLE_TILE, SS0)
            pool_rest(pool)

        @block.vector
        def _(v):
            v.wait_ge(par_ld, 32)
            v.wait_ge(x_ld, 16)
            for b in range(0, KB, 4):
                v.tensor_scalar(X[:, b:b + 4, :], X[:, b:b + 4, :], ALPHA, None, ALU.mult).then_inc(x_scaled, 1)
            n_ln = KB * (NSUB - 1)
            for c in (P_LNG, P_LNB):
                v.tensor_scalar(PAR[:, c:c + n_ln], PAR[:, c:c + n_ln], ALPHA, None, ALU.mult).then_inc(x_scaled, 1)
            vec_ada(v)
            v.wait_ge(x_scaled, 4)
            every(vec_hin_chunk(v, 0, 0))
            with v.Fori(0, QKVB // 2) as i:
                for u in range(2):
                    n = 2 * i + u
                    need(v, pst_rdy, n + 1)
                    need(v, up_ev, 3 * n + 3)
                    need(v, v_done, n - 1)
                    src = lambda j: UB[u][:, GAP - (GC - 1) + j:GAP - (GC - 1) + j + T]
                    v.tensor_scalar(CV[u][:, :], src(0), PST[:, u, 0:1], None, ALU.mult).then_inc(vec_ch, 1)
                    for j in range(1, GC):
                        v.wait_ge(vec_ch, n * (GC - 1) + j)
                        v.scalar_tensor_tensor(CV[u][:, :], src(j), PST[:, u, j:j + 1], CV[u][:, :], ALU.mult, ALU.add)\
                            .then_inc(vec_ch if j < GC - 1 else conv_done, 1)
                    vec_ada_sums(v, n, u, i, False)
            with v.Fori(QKVB // 2, (QKVB + ZB) // 2) as i:
                for u in range(2):
                    vec_ada_sums(v, 2 * i + u, u, i, True)
            need(v, ada_sum, QKVB + ZB)
            vec_ada_constants(v, 1, NSUB)
            v.wait_ge(ada_done, 5)
            need(v, ab_ps, 1)
            need(v, gx, 1)
            shp = [128, GT + 1, 8]
            v.tensor_tensor(GX[:, 0], PS[:, 0, 0:(GT + 1) * 16].rearrange("p (t c) -> p t c", c=16)[:, :, 8:16],
                            PAR[:, P_DTB:P_DTB + 8].unsqueeze(1).to_broadcast(shp), ALU.add).then_inc(bg_rdy, 1)
            need(v, bg_rdy, 1)
            v.tensor_scalar(GX[:, 1], GX[:, 0], 0.0, None, ALU.min).then_inc(bg_rdy, 1)
            v.tensor_scalar(GX[:, 3], GX[:, 0], 0.0, None, ALU.max).then_inc(bg_rdy, 1)
            need(v, bg_rdy, 3)
            v.tensor_tensor(GX[:, 1], GX[:, 1], GX[:, 3], ALU.subtract).then_inc(bg_rdy, 1)
            need(v, gx, 4)
            v.tensor_tensor(GX[:, 0], GX[:, 3], GX[:, 2], ALU.add).then_inc(bg_rdy, 1)
            need(v, bg_rdy, 5)
            v.scalar_tensor_tensor(BETAG[:, :, 0:8], GX[:, 0], -1.0, AL[:, :].unsqueeze(1).to_broadcast(shp), ALU.mult, ALU.mult).then_inc(bg_rdy, 1)
            need(v, bg_rdy, 6)
            with v.Fori(0, GT) as i:
                vec_g(v, i, PROMPT_TILE, SP0)
            vec_g(v, GT, SAMPLE_TILE, SS0)
            vec_rest(v)

        @block.tensor
        def _(pe):
            pe.wait_ge(sc_done, 1)
            pe_ada(pe)

            def body(i, z, ready=None):
                for u in range(2):
                    dense(pe, 2 * i + u, u, 2 * i + u, u, ready if u == 0 else None)
            body(0, False, hin_ready(pe, 0))
            with pe.Fori(1, QKVB // 2) as i:
                body(i, False)
            with pe.Fori(QKVB // 2, (QKVB + ZB) // 2) as i:
                body(i, True)
            dense(pe, QKVB + ZB, 0, QKVB + ZB, 0)
            need(pe, up_ev, 3 * (QKVB + ZB + 1))
            for t in range(GT + 1):
                mm = pe.transpose(PS[:, 0, t * 16:t * 16 + 16], AB[0:16, tile_start(t):tile_start(t) + 128], CST[0:16, C_ID, 0:16])
            mm.then_inc(ab_ps, 1)
            with pe.Fori(0, GT) as i:
                pe_g(pe, i, PROMPT_TILE, SP0)
            need(pe, s0_ld, 16)
            pe_g(pe, GT, SAMPLE_TILE, SS0)
            pe_rest(pe)


_INS = ["xT", "cT", "cB", "ws", "wada0", "wada", "par", "cst", "s0", "cs", "rows", "msk", "pckv", "pkpe"]
_OUTS = [("y", (128, KB, T)), ("o_gdn", (128, HEADS, 128)), ("o_gcv", (128, QKVB, 2, GC - 1)), ("s_gdn", (128, HEADS, 128)),
         ("o_fcv", (DEPTH, 128, FB, 2, 2, 2)), ("o_ckv", (128, LB, T)), ("o_kpe", (ROPE, T))]


def pack(i):
    import numpy as np
    f = lambda a: np.asarray(a, np.float32) if a.dtype != np.float32 else a
    A = {k: np.asarray(v) for k, v in i.items()}
    xT = np.zeros((T, D), np.float32)
    xT[:SEQ] = A["x_prompt"][0]
    xT[SAM:] = A["x_sample"][0]
    fm = lambda a: np.ascontiguousarray(a.reshape(a.shape[0], -1, 128).transpose(2, 1, 0))
    c = np.concatenate([A["c_prompt"], A["c_sample"]])
    cT = fm(c)
    cB = np.ascontiguousarray(np.broadcast_to(c[None], (128,) + c.shape))

    ws = np.zeros((NSLAB, 128, SLAB), np.float32)

    def cols(w):
        k, m = w.shape
        return w.reshape(k // 128, 128, m // 128, 128).transpose(2, 1, 0, 3).reshape(m // 128, 128, k)

    def put(n, s):
        ws[n:n + s.shape[0], :, :s.shape[2]] = s
    win = np.zeros((D, (QKVB + ZB + 1) * 128), np.float32)
    win[:, :A["gdn_w_in"].shape[2]] = A["gdn_w_in"][0]
    put(S_A, cols(win))
    put(S_WO, cols(A["gdn_w_out"][0]))
    for l, s in ((0, S_F0), (1, S_F1)):
        up = cols(A["ffn_w_in"][l])
        down = A["ffn_w_down"][l].reshape(FB // 2, 2, 128, 2, 512).transpose(0, 3, 2, 1, 4).reshape(FB, 128, SLAB)
        order = []
        for j in range(FB // 2):
            a0, b0, a1, b1 = up[2 * j], up[FB + 2 * j], up[2 * j + 1], up[FB + 2 * j + 1]
            order += [a0, b0] + ([down[2 * j - 2], down[2 * j - 1]] if j else []) + [a1, b1]
        order += [down[FB - 2], down[FB - 1]]
        put(s, np.stack(order))
    kvd = A["kv_w_down"]
    put(S_KV, cols(np.concatenate([kvd, kvd[:, 256:]], 1)))
    put(S_DQ, cols(A["mla_w_dq"][0]))
    uq = A["mla_w_uq"][0].reshape(384, HEADS, 192)
    qp = cols(np.ascontiguousarray(uq[:, :, 128:]).reshape(384, HEADS * 64))
    put(S_QP, np.concatenate([qp[0::2], qp[1::2]], 2))
    up = A["kv_w_up"].reshape(256, HEADS, 256)
    qn = cols(np.ascontiguousarray(uq[:, :, :128]).reshape(384, HEADS * 128))
    kn = cols(np.ascontiguousarray(up[:, :, :128]).reshape(256, HEADS * 128))
    vn = cols(np.ascontiguousarray(up[:, :, 128:]).reshape(256, HEADS * 128))
    put(S_HD, np.concatenate([qn, kn, vn], 2))
    put(S_MO, cols(A["mla_w_out"][0]))
    wada0 = np.ascontiguousarray(cols(A["ada_w"][0]).transpose(1, 0, 2))
    wada = np.ascontiguousarray(A["ada_w"][1:].transpose(0, 2, 1)).reshape((NSUB - 1) * ADAM, 128, D)

    par = np.zeros((128, NPAR), np.float32)
    blk = lambda a: a.reshape(-1, 128).T
    par[:, P_ADAB:P_LNG] = blk(A["ada_b"])
    par[:, P_LNG:P_LNB] = blk(A["ln_g"])
    par[:, P_LNB:P_GCV] = blk(A["ln_b"])
    g = np.concatenate([A["gdn_conv_w"][0], A["state_gdn_conv"][0, 0]])
    par[:, P_GCV:P_FFN] = g.reshape(GPW, QKVB, 128).transpose(2, 1, 0).reshape(128, -1)
    for l in range(DEPTH):
        g = np.concatenate([A["ffn_b_in"][l:l + 1], A["ffn_conv_w"][l], A["ffn_conv_b"][l:l + 1], A["state_ffn_conv"][0, l]])
        g = g.reshape(7, 2, FB, 128).transpose(3, 2, 1, 0).reshape(128, -1)
        par[:, P_FFN + l * FB * FPW:P_FFN + (l + 1) * FB * FPW] = g
    par[:, P_GNG] = A["gdn_norm_g"][0]
    par[:, P_KVG:P_QG] = blk(A["kv_norm_g"])
    par[:, P_QG:P_ALOG] = blk(A["mla_q_norm_g"][0])
    par[:, P_ALOG:P_DTB] = A["gdn_a_log"][0][None, :]
    par[:, P_DTB:] = A["gdn_dt_bias"][0][None, :]
    cs, rows, msk = tables()
    ck = A["cache_ckv"][0]
    kp = A["cache_kpe"][0].T
    return {"cs": cs, "rows": rows, "msk": msk, "pckv": fm(ck), "pkpe": np.concatenate([kp, kp]), "xT": fm(xT), "cT": cT, "cB": cB, "ws": ws, "wada0": wada0, "wada": wada, "par": par, "cst": constants(),
            "s0": np.ascontiguousarray(A["state_gdn"][0, 0].transpose(1, 0, 2))}


def unpack(r):
    import numpy as np
    tok = lambda a: a.transpose(2, 1, 0).reshape(a.shape[2], -1)
    y = tok(r["y"])
    g = r["o_gcv"].transpose(2, 3, 1, 0).reshape(2, 1, 1, GC - 1, -1)
    f = r["o_fcv"].transpose(4, 0, 5, 3, 2, 1).reshape(2, 1, DEPTH, FC - 1, -1)
    ckv, kpe = tok(r["o_ckv"]), r["o_kpe"].T
    return (y[None, :SEQ], y[None, SAM:], r["o_gdn"].transpose(1, 0, 2)[None, None], g[0], f[0], ckv[None, :SEQ], kpe[None, :SEQ],
            r["s_gdn"].transpose(1, 0, 2)[None, None], g[1], f[1], ckv[None, SAM:], kpe[None, SAM:])


def kernel(**inputs):
    import numpy as np
    import concourse.bacc as bacc
    from concourse.bass_utils import run_bass_kernel_spmd
    arrays = pack(inputs)
    nc = bacc.Bacc("TRN2", target_bir_lowering=False, num_devices=1)
    args = [nc.dram_tensor(n, arrays[n].shape, mybir.dt.float32, kind="ExternalInput").ap() for n in _INS]
    args += [nc.dram_tensor(n, s, mybir.dt.float32, kind="ExternalOutput").ap() for n, s in _OUTS]
    build(nc, *args)
    r = run_bass_kernel_spmd(nc, [arrays], core_ids=[0]).results[0]
    return unpack(r)
```
